# Optimizing a Trainium2 kernel written in Bass

```python
import jax, jax.numpy as jnp
from jax import lax
import numpy as np

D_MODEL = 1024
BATCH = 1
SEQ = 256
DEPTH = 2

NSA_HEADS = 8
NSA_KV_HEADS = 2
HEAD_DIM = 64
HPG = NSA_HEADS // NSA_KV_HEADS
CMP_LEN = 32
CMP_STRIDE = 16
CMP_HIDDEN = 256
SEL_LEN = 64
N_SEL = 16
WINDOW = 512
Q_BLOCK = 128
NSA_WIDTH = NSA_HEADS * HEAD_DIM
CONV_CH = D_MODEL // 2
CONV_WIDTH = 31
Q_COLS = NSA_WIDTH
KV_COLS = 3 * 2 * NSA_KV_HEADS * HEAD_DIM
GATE_COLS = 3 * NSA_HEADS
IN0_COLS = Q_COLS + KV_COLS + GATE_COLS + 2 * CONV_CH
MIX0_WIDTH = NSA_WIDTH + CONV_CH
GMLP_WIDTH = D_MODEL
GMLP_GROUPS = 8
GMLP_CHUNK = 128
DENSE_FF = 2816
N_EXPERTS = 8
TOP_K = 2
EXPERT_FF = 3584
MOE_BLOCK = 256
EPS = 1e-6
N_EVEN = (DEPTH + 1) // 2
N_ODD = DEPTH // 2

kernel_name = 'hybrid_nsa_conformer_gmlp_moe'

def rms_norm(x, g):
    xf = x.astype(jnp.float32)
    y = xf * lax.rsqrt(jnp.mean(xf * xf, axis=-1, keepdims=True) + EPS)
    return (y * g.astype(jnp.float32)).astype(x.dtype)

def layer_norm(x, g, b):
    xf = x.astype(jnp.float32)
    mu = jnp.mean(xf, axis=-1, keepdims=True)
    xc = xf - mu
    var = jnp.mean(xc * xc, axis=-1, keepdims=True)
    return (xc * lax.rsqrt(var + EPS) * g.astype(jnp.float32) + b.astype(jnp.float32)).astype(x.dtype)

def masked_softmax(s, mask, axis):
    s = jnp.where(mask, s.astype(jnp.float32), -1e30)
    return jax.nn.softmax(s, axis=axis)

def swiglu(x, w_gate, w_up, w_down):
    return (jax.nn.silu(x @ w_gate) * (x @ w_up)) @ w_down

def compress_blocks(k, pe, w1, b1, w2, b2):
    S = k.shape[2]
    nc = (S - CMP_LEN) // CMP_STRIDE + 1
    idx = np.arange(nc)[:, None] * CMP_STRIDE + np.arange(CMP_LEN)[None, :]
    blocks = k[:, :, idx] + pe
    flat = blocks.reshape(blocks.shape[:3] + (CMP_LEN * HEAD_DIM,))
    return jax.nn.gelu(flat @ w1 + b1) @ w2 + b2

def nsa_attention(q, k_cmp, v_cmp, k_slc, v_slc, k_win, v_win, gates,
                  cmp_pe, cmp_w1, cmp_b1, cmp_w2, cmp_b2):
    B, G, Hg, S, hd = q.shape
    scale = hd ** -0.5
    t = jnp.arange(S)

    kc = compress_blocks(k_cmp, cmp_pe[0], cmp_w1[0], cmp_b1[0], cmp_w2[0], cmp_b2[0])
    vc = compress_blocks(v_cmp, cmp_pe[1], cmp_w1[1], cmp_b1[1], cmp_w2[1], cmp_b2[1])
    nc = kc.shape[2]
    c_end = jnp.arange(nc) * CMP_STRIDE + CMP_LEN - 1
    c_mask = c_end[None, :] <= t[:, None]
    s_c = jnp.einsum('bghtd,bgnd->bghtn', q, kc) * scale
    p_c = jnp.where(c_mask, masked_softmax(s_c, c_mask, -1), 0.0)
    o_c = jnp.einsum('bghtn,bgnd->bghtd', p_c.astype(vc.dtype), vc)

    nsb = S // SEL_LEN
    cs = np.arange(nc) * CMP_STRIDE
    js = np.arange(nsb) * SEL_LEN
    overlap = jnp.asarray(((cs[:, None] < js[None, :] + SEL_LEN) &
                           (cs[:, None] + CMP_LEN > js[None, :])).astype(np.float32))
    imp = jnp.einsum('bghtn,nj->bgtj', p_c, overlap)
    blk = jnp.arange(nsb)[None, :]
    cur = (t // SEL_LEN)[:, None]
    valid = blk <= cur
    forced = (blk == 0) | (blk == cur) | (blk == cur - 1)
    score = jnp.where(valid, imp + jnp.where(forced, 1e6, 0.0), -1e9)
    n_sel = min(N_SEL, nsb)
    _, sel = lax.top_k(score, n_sel)

    nqb = S // Q_BLOCK
    kb = k_slc.reshape(B, G, nsb, SEL_LEN, hd)
    vb = v_slc.reshape(B, G, nsb, SEL_LEN, hd)
    gather = jax.vmap(jax.vmap(lambda blocks, ids: blocks[ids]))
    q_blocks = jnp.moveaxis(q.reshape(B, G, Hg, nqb, Q_BLOCK, hd), 3, 0)
    sel_blocks = jnp.moveaxis(sel.reshape(B, G, nqb, Q_BLOCK, n_sel), 2, 0)
    t_blocks = t.reshape(nqb, Q_BLOCK)

    def sel_block(args):
        qb, sb, tb = args
        kg = gather(kb, sb)
        vg = gather(vb, sb)
        s = jnp.einsum('bghqd,bgqnld->bghqnl', qb, kg) * scale
        kpos = sb[..., None] * SEL_LEN + jnp.arange(SEL_LEN)
        mask = (kpos <= tb[None, None, :, None, None])[:, :, None]
        p = masked_softmax(s, mask, (-2, -1))
        return jnp.einsum('bghqnl,bgqnld->bghqd', p.astype(vg.dtype), vg)

    o_s = lax.map(sel_block, (q_blocks, sel_blocks, t_blocks))
    o_s = jnp.moveaxis(o_s, 0, 3).reshape(B, G, Hg, S, hd)

    kp = jnp.pad(k_win, ((0, 0), (0, 0), (WINDOW, 0), (0, 0)))
    vp = jnp.pad(v_win, ((0, 0), (0, 0), (WINDOW, 0), (0, 0)))
    widx = np.arange(nqb)[:, None] * Q_BLOCK + np.arange(Q_BLOCK + WINDOW)[None, :]
    kw = kp[:, :, widx]
    vw = vp[:, :, widx]
    qw = q.reshape(B, G, Hg, nqb, Q_BLOCK, hd)
    s_w = jnp.einsum('bghnqd,bgnkd->bghnqk', qw, kw) * scale
    kpos = jnp.asarray(widx - WINDOW)[:, None, :]
    qpos = t_blocks[:, :, None]
    w_mask = (kpos <= qpos) & (kpos > qpos - WINDOW) & (kpos >= 0)
    p_w = masked_softmax(s_w, w_mask, -1)
    o_w = jnp.einsum('bghnqk,bgnkd->bghnqd', p_w.astype(vw.dtype), vw).reshape(B, G, Hg, S, hd)

    return gates[..., 0:1] * o_c + gates[..., 1:2] * o_s + gates[..., 2:3] * o_w

def mixer_nsa_conv(u, w_in, cmp_pe, cmp_w1, cmp_b1, cmp_w2, cmp_b2,
                   conv_w, conv_b, conv_ln_g, conv_ln_b, w_out):
    B, S, _ = u.shape
    proj = u @ w_in
    q, kv, g, glu = jnp.split(proj, [Q_COLS, Q_COLS + KV_COLS, Q_COLS + KV_COLS + GATE_COLS], axis=-1)
    q = q.reshape(B, S, NSA_KV_HEADS, HPG, HEAD_DIM).transpose(0, 2, 3, 1, 4)
    kv = kv.reshape(B, S, 6, NSA_KV_HEADS, HEAD_DIM).transpose(2, 0, 3, 1, 4)
    gates = jax.nn.sigmoid(g.reshape(B, S, NSA_KV_HEADS, HPG, 3).transpose(0, 2, 3, 1, 4))
    o = nsa_attention(q, kv[0], kv[1], kv[2], kv[3], kv[4], kv[5], gates,
                      cmp_pe, cmp_w1, cmp_b1, cmp_w2, cmp_b2)
    o_attn = o.transpose(0, 3, 1, 2, 4).reshape(B, S, NSA_WIDTH)
    a, b = jnp.split(glu, 2, axis=-1)
    c = a * jax.nn.sigmoid(b)
    c = lax.conv_general_dilated(c, conv_w, window_strides=(1,), padding=[(CONV_WIDTH - 1, 0)],
                                 dimension_numbers=('NWC', 'WIO', 'NWC'),
                                 feature_group_count=CONV_CH) + conv_b
    c = jax.nn.silu(layer_norm(c, conv_ln_g, conv_ln_b))
    return jnp.concatenate([o_attn, c], axis=-1) @ w_out

def mixer_gmlp(u, w_in, ln_g, ln_b, w_s, b_s, w_out):
    B, S, _ = u.shape
    z = jax.nn.gelu(u @ w_in)
    z1, z2 = jnp.split(z, 2, axis=-1)
    z2 = layer_norm(z2, ln_g, ln_b)
    nch = S // GMLP_CHUNK
    z2 = z2.reshape(B, nch, GMLP_CHUNK, GMLP_GROUPS, GMLP_WIDTH // GMLP_GROUPS)
    causal = jnp.tril(jnp.ones((GMLP_CHUNK, GMLP_CHUNK), dtype=bool))
    ws = jnp.where(causal, w_s, 0.0)
    mixed = jnp.einsum('gts,bcsgd->bctgd', ws, z2) + b_s.T[:, :, None]
    return (z1 * mixed.reshape(B, S, GMLP_WIDTH)) @ w_out

def moe_swiglu(x, w_router, w_gate, w_up, w_down):
    B, S, D = x.shape
    h = x.reshape(-1, D)
    n = h.shape[0]
    logits = (h @ w_router).astype(jnp.float32)
    top_logit, top_e = lax.top_k(logits, TOP_K)
    top_w = jax.nn.softmax(top_logit, axis=-1)
    nk = n * TOP_K
    e_flat = top_e.reshape(-1)
    w_flat = top_w.reshape(-1)
    tok_flat = jnp.arange(nk) // TOP_K
    order = jnp.argsort(e_flat)
    e_sorted = e_flat[order]
    counts = jnp.zeros((N_EXPERTS,), jnp.int32).at[e_flat].add(1)
    starts = jnp.cumsum(counts) - counts
    padded = (counts + MOE_BLOCK - 1) // MOE_BLOCK * MOE_BLOCK
    pad_ends = jnp.cumsum(padded)
    pad_starts = pad_ends - padded
    dest = pad_starts[e_sorted] + (jnp.arange(nk) - starts[e_sorted])
    n_rows = nk + N_EXPERTS * MOE_BLOCK
    n_blocks = n_rows // MOE_BLOCK
    row_tok = jnp.full((n_rows,), n, jnp.int32).at[dest].set(tok_flat[order])
    row_w = jnp.zeros((n_rows,), jnp.float32).at[dest].set(w_flat[order])
    block_e = jnp.minimum(jnp.searchsorted(pad_ends, jnp.arange(n_blocks) * MOE_BLOCK, side='right'),
                          N_EXPERTS - 1)
    h_pad = jnp.concatenate([h, jnp.zeros((1, D), h.dtype)], axis=0)
    xb = h_pad[row_tok].reshape(n_blocks, MOE_BLOCK, D)

    def expert_block(args):
        xe, e = args
        return swiglu(xe, w_gate[e], w_up[e], w_down[e])

    yb = lax.map(expert_block, (xb, block_e)).reshape(n_rows, D)
    out = jnp.zeros((n + 1, D), jnp.float32).at[row_tok].add(yb.astype(jnp.float32) * row_w[:, None])
    return out[:n].astype(x.dtype).reshape(B, S, D)

def setup_inputs(seed: int = 0) -> dict:
    key = jax.random.key(seed)
    keys = jax.random.split(key, 32)
    D = D_MODEL
    NE = N_EVEN
    NO = N_ODD

    def nrm(i, shape, scale):
        return jax.random.normal(keys[i], shape, jnp.float32) * scale

    return {
        'x': nrm(0, (BATCH, SEQ, D), 1.0),
        'norm_mix_pre': 1.0 + nrm(1, (DEPTH, D), 0.02),
        'norm_mix_post': 1.0 + nrm(2, (DEPTH, D), 0.02),
        'norm_ffn_pre': 1.0 + nrm(3, (DEPTH, D), 0.02),
        'norm_ffn_post': 1.0 + nrm(4, (DEPTH, D), 0.02),
        'nsa_conv_w_in': nrm(5, (NE, D, IN0_COLS), D ** -0.5),
        'cmp_pe': nrm(6, (NE, 2, CMP_LEN, HEAD_DIM), 0.1),
        'cmp_w1': nrm(7, (NE, 2, CMP_LEN * HEAD_DIM, CMP_HIDDEN), (CMP_LEN * HEAD_DIM) ** -0.5),
        'cmp_b1': nrm(8, (NE, 2, CMP_HIDDEN), 0.01),
        'cmp_w2': nrm(9, (NE, 2, CMP_HIDDEN, HEAD_DIM), CMP_HIDDEN ** -0.5),
        'cmp_b2': nrm(10, (NE, 2, HEAD_DIM), 0.01),
        'conv_w': nrm(11, (NE, CONV_WIDTH, 1, CONV_CH), CONV_WIDTH ** -0.5),
        'conv_b': nrm(12, (NE, CONV_CH), 0.01),
        'conv_ln_g': 1.0 + nrm(13, (NE, CONV_CH), 0.02),
        'conv_ln_b': nrm(14, (NE, CONV_CH), 0.01),
        'nsa_conv_w_out': nrm(15, (NE, MIX0_WIDTH, D), MIX0_WIDTH ** -0.5),
        'ffn_w_gate': nrm(16, (NE, D, DENSE_FF), D ** -0.5),
        'ffn_w_up': nrm(17, (NE, D, DENSE_FF), D ** -0.5),
        'ffn_w_down': nrm(18, (NE, DENSE_FF, D), DENSE_FF ** -0.5),
        'gmlp_w_in': nrm(19, (NO, D, 2 * GMLP_WIDTH), D ** -0.5),
        'gmlp_ln_g': 1.0 + nrm(20, (NO, GMLP_WIDTH), 0.02),
        'gmlp_ln_b': nrm(21, (NO, GMLP_WIDTH), 0.01),
        'gmlp_w_s': nrm(22, (NO, GMLP_GROUPS, GMLP_CHUNK, GMLP_CHUNK), GMLP_CHUNK ** -0.5),
        'gmlp_b_s': 1.0 + nrm(23, (NO, GMLP_GROUPS, GMLP_CHUNK), 0.01),
        'gmlp_w_out': nrm(24, (NO, GMLP_WIDTH, D), GMLP_WIDTH ** -0.5),
        'moe_w_router': nrm(25, (NO, D, N_EXPERTS), D ** -0.5),
        'moe_w_gate': nrm(26, (NO, N_EXPERTS, D, EXPERT_FF), D ** -0.5),
        'moe_w_up': nrm(27, (NO, N_EXPERTS, D, EXPERT_FF), D ** -0.5),
        'moe_w_down': nrm(28, (NO, N_EXPERTS, EXPERT_FF, D), EXPERT_FF ** -0.5),
    }

def reference(x, norm_mix_pre, norm_mix_post, norm_ffn_pre, norm_ffn_post,
              nsa_conv_w_in, cmp_pe, cmp_w1, cmp_b1, cmp_w2, cmp_b2,
              conv_w, conv_b, conv_ln_g, conv_ln_b, nsa_conv_w_out,
              ffn_w_gate, ffn_w_up, ffn_w_down,
              gmlp_w_in, gmlp_ln_g, gmlp_ln_b, gmlp_w_s, gmlp_b_s, gmlp_w_out,
              moe_w_router, moe_w_gate, moe_w_up, moe_w_down):
    h = x
    for layer in range(DEPTH):
        i = layer // 2
        u = rms_norm(h, norm_mix_pre[layer])
        if layer % 2 == 0:
            m = mixer_nsa_conv(u, nsa_conv_w_in[i], cmp_pe[i], cmp_w1[i], cmp_b1[i], cmp_w2[i], cmp_b2[i],
                               conv_w[i], conv_b[i], conv_ln_g[i], conv_ln_b[i], nsa_conv_w_out[i])
        else:
            m = mixer_gmlp(u, gmlp_w_in[i], gmlp_ln_g[i], gmlp_ln_b[i], gmlp_w_s[i], gmlp_b_s[i], gmlp_w_out[i])
        h = h + rms_norm(m, norm_mix_post[layer])
        u = rms_norm(h, norm_ffn_pre[layer])
        if layer % 2 == 0:
            f = swiglu(u, ffn_w_gate[i], ffn_w_up[i], ffn_w_down[i])
        else:
            f = moe_swiglu(u, moe_w_router[i], moe_w_gate[i], moe_w_up[i], moe_w_down[i])
        h = h + rms_norm(f, norm_ffn_post[layer])
    return h


_drawn_inputs = setup_inputs


def setup_inputs(seed=0):
    import zlib

    import numpy as np

    out = dict(_drawn_inputs(seed))
    spreads = {}
    factors = {'cmp_b1': 8.0,
     'cmp_b2': 2.83,
     'gmlp_ln_g': 64.0,
     'gmlp_ln_b': 190.096,
     'gmlp_b_s': 64.0,
     'conv_ln_b': 3.02}
    for name, (base, spread) in spreads.items():
        noise = np.random.default_rng([zlib.crc32(name.encode()), seed]).standard_normal(out[name].shape)
        drawn = base * np.exp(spread * noise) if base else spread * noise
        out[name] = __import__('jax').numpy.asarray(drawn.astype(out[name].dtype))
    for name, factor in factors.items():
        out[name] = (out[name] * factor).astype(out[name].dtype)
    return out
```

```python
from contextlib import ExitStack

import concourse.bass as bass
from concourse import mybir

F32 = mybir.dt.float32
F32R = mybir.dt.float32r
I32 = mybir.dt.int32
ALU = mybir.AluOpType
ACT = mybir.ActivationFunctionType
AX = mybir.AxisListType

P = 128
T = 2
S = T * P
D = 1024
KC = D // P
HEADS, KV_HEADS, HD = 8, 2, 64
HPG = HEADS // KV_HEADS
QC = HEADS * HD
KVC = 3 * 2 * KV_HEADS * HD
GATES = 3 * HEADS
CONV_CH, CONV_W = 512, 31
CC = CONV_CH // P
CMP_LEN, CMP_STRIDE, CMP_HID = 32, 16, 256
NCMP = (S - CMP_LEN) // CMP_STRIDE + 1
NG = KV_HEADS * NCMP
FF = 2816
FFN_BLOCKS = FF // 256
GM = 1024
NE = 8
EFF = 3584
MOE_BLOCKS = EFF // 512
ONE_TILE = P
EPS = 1e-6
NEG = -1e30

UF = 2048
SLOTS = 14
RING1 = 9
RING2 = 12
SCRATCH = SLOTS - RING1
PARTS = 3
U_GLU, U_CMP_IN, U_Q, U_SLC, U_WIN, U_CW1, U_OUT0 = 0, 4, 5, 7, 8, 9, 13
U_FFN = 17
U_GM = U_FFN + 3 * FFN_BLOCKS
U_GMO = U_GM + 8
U_MOE = U_GMO + 4
MOE_UNITS = 6 * MOE_BLOCKS
HIDDEN = (1, 3)
FFN_LOOP0 = 2
assert 2 * MOE_UNITS % RING2 == 0 and MOE_UNITS % PARTS == 0 and 9 % RING1 == 0 and 9 % PARTS == 0

V_MIX, V_FFN, V_CB, V_CG, V_CLB, V_B1, V_PE, V_BS, V_B2K = 0, 16, 32, 36, 40, 44, 48, 80, 88
V_ROWS = 89
VEC_LOADS = 11
SMALL_LOADS = 5


def moe_slot(m):
    m %= RING2
    new = RING2 - RING1
    return RING1 + m if m < new else (U_MOE + m - new) % RING1


def unit_dmas(k):
    if U_FFN <= k < U_GM:
        j = k - U_FFN
        return 1 if j == 32 or (j >= 4 and (j - 2) % 3 == 2) else 2
    return 1


def raw_slot(k):
    return k % RING1 if k < U_MOE else moe_slot(k - U_MOE)


def raw_count(k):
    return 16 * sum(unit_dmas(i) for i in range(k % RING1, k + 1, RING1))


def moe_count(m):
    s = moe_slot(m)
    before = 0 if s >= RING1 else raw_count(max(k for k in range(U_MOE) if k % RING1 == s))
    return before + 16 * (m // RING2 + 1)


def program(nc, x, norm_mix_pre, norm_mix_post, norm_ffn_pre, norm_ffn_post, nsa_conv_w_in, cmp_pe,
            cmp_w1, cmp_b1, cmp_w2, cmp_b2, conv_w, conv_b, conv_ln_g, conv_ln_b, nsa_conv_w_out,
            ffn_w_gate, ffn_w_up, ffn_w_down, gmlp_w_in, gmlp_ln_g, gmlp_ln_b, gmlp_w_s, gmlp_b_s,
            gmlp_w_out, moe_w_router, moe_w_gate, moe_w_up, moe_w_down, out):
    ctx = ExitStack()
    with ctx:
        def sb(name, shape, dt=F32):
            return ctx.enter_context(nc.sbuf_tensor(name, shape, dt))

        def sem(name):
            return ctx.enter_context(nc.semaphore(name))

        raw = sb("raw", [P, SLOTS, UF])
        w_hi = sb("w_hi", [P, PARTS, UF], F32R)
        w_lo = sb("w_lo", [P, PARTS, UF], F32R)
        xres = sb("xres", [P, T, D])
        xn = sb("xn", [P, T, D])
        gpost = sb("gpost", [P, D])
        ra = sb("ra", [P, 4 * 1024], F32R)
        ht = sb("ht", [P, 2, 1024], F32R)
        pt01 = sb("pt01", [P, 2, S], F32R)
        ident = sb("ident", [P, P])
        vec = sb("vec", [P, V_ROWS])
        st = sb("st", [P, 80])
        neg_half = sb("neg_half", [P, 2])
        flag = sb("flag", [P, 2 * NE + 1], I32)
        ps = ctx.enter_context(nc.psum_tensor("ps", [P, 8, 512], F32))

        uT_h = ra[:, 0:2048].rearrange("p (c t) -> p c t", c=KC)
        uT_l = ra[:, 2048:4096].rearrange("p (c t) -> p c t", c=KC)

        area = raw[:, RING1:SLOTS, :].rearrange("p s f -> p (s f)")
        at = [0]

        def take(n):
            at[0] += n
            assert at[0] <= SCRATCH * UF
            return area[:, at[0] - n:at[0]]

        prob = take(2048)
        probT = take(1024)
        qT = take(1024).rearrange("p (c t) -> p c t", c=4)
        kT = [take(512).rearrange("p (g t) -> p g t", g=2) for _ in range(2)]
        vv = [take(256).rearrange("p (t n) -> p t n", t=T) for _ in range(2)]
        PADT = CONV_W - 1 + S
        cT = take(CC * PADT).rearrange("p (c t) -> p c t", c=CC)
        yT = take(CC * S).rearrange("p (c t) -> p c t", c=CC)
        mask = take(S)
        vec_rows = take(P)
        cw_rows = take(P)
        cw = take(CC * CONV_W)
        w2k = take(256).rearrange("p (h n) -> p h n", h=2)
        w2v = take(128).rearrange("p (h n) -> p h n", h=2)
        wgate = take(KC * GATES)
        gates = take(T * GATES).rearrange("p (t n) -> p t n", t=T)
        hc = take(4 * NG).rearrange("p (k h n) -> p k h n", k=2, h=2)
        kcT = take(NG)
        vc = take(2 * HD).rearrange("p (g d) -> p g d", g=2)
        b2v = take(HD)
        cadd = take(2 * NCMP).rearrange("p (i n) -> p i n", i=2)
        cmul = take(2 * NCMP).rearrange("p (i n) -> p i n", i=2)
        ptmp = take(S)
        atmp = take(S)
        both = take(2 * P).rearrange("p (g n) -> p g n", g=2)
        ktmp = prob[:, 0:4 * S].rearrange("p (k t) -> p k t", k=4)
        xcmp = probT[:, 0:4 * 240].rearrange("p (k c g n) -> p k c g n", k=2, c=16, g=2)
        xc_h = ra[:, 0:960].rearrange("p (k c n) -> p k c n", k=2, c=16)
        xc_l = ra[:, 1024:1984].rearrange("p (k c n) -> p k c n", k=2, c=16)
        y2 = cT[:, :, 0:S]
        hnat = prob[:, 1024:1536].rearrange("p (k n) -> p k n", k=2)
        pcT = prob[:, 0:2048].rearrange("p (q t) -> p q t", q=16)
        oacc = xn[:, 0, :].rearrange("p (i n) -> p i n", i=T)
        cn = xn[:, 1, :].rearrange("p (i n) -> p i n", i=T)

        z1 = area[:, 0:2048].rearrange("p (t n) -> p t n", t=T)
        z2 = area[:, 2048:4096].rearrange("p (t n) -> p t n", t=T)
        ws = area[:, 4096:5120].rearrange("p (g s) -> p g s", g=8)
        wsT = area[:, 5120:6144].rearrange("p (g s) -> p g s", g=8)
        ln_g = area[:, 6144:7168]
        ln_b = area[:, 7168:8192]

        sg, hbuf = area[:, 8192:8704], area[:, 8704:9216]
        iota, tri, ones = area[:, 6144:6400], area[:, 6400:6528], area[:, 6528:6656]
        sel01 = area[:, 7168:7680].rearrange("p (t j) -> p t j", t=T)
        selr = area[:, 7680:8192].rearrange("p (t j) -> p t j", t=T)
        esg = area[:, 8192:9216].rearrange("p (i n) -> p i n", i=2)
        eh = area[:, 9216:10240].rearrange("p (i n) -> p i n", i=2)
        router = gpost[:, 512:576].rearrange("p (c e) -> p c e", c=KC)
        rt = gpost[:, 576:1024]
        acc = xn

        def y_part(part, i, q):
            if i:
                return ht[:, part, 512 * q:512 * q + 512]
            return ra[:, 2048 * part + 1024 + 512 * q:2048 * part + 1536 + 512 * q]

        raw_in = [sem(f"raw_in{i}") for i in range(SLOTS)]
        hi_done, lo_done, unit_used = sem("hi_done"), sem("lo_done"), sem("unit_used")
        x_in, vec_in, small_in, post_in, gm_in = sem("x_in"), sem("vec_in"), sem("small_in"), sem("post_in"), sem("gm_in")
        router_in, stored = sem("router_in"), sem("stored")
        consts, vec_ps, vec_sb = sem("consts"), sem("vec_ps"), sem("vec_sb")
        ss_done, xn_done, xT_ps = sem("ss_done"), sem("xn_done"), sem("xT_ps")
        uh_done, ul_done, x_new = sem("uh_done"), sem("ul_done"), sem("x_new")
        ws_in, route_consts = sem("ws_in"), sem("route_consts")
        dup_ps, rs_in, rs_out = sem("dup_ps"), sem("rs_in"), sem("rs_out")
        wg_hi, wg_lo, gates_ps = sem("wg_hi"), sem("wg_lo"), sem("gates_ps")
        proj_sb, xcmp_sb, glu_sig, glu_sb = sem("proj_sb"), sem("xcmp_sb"), sem("glu_sig"), sem("glu_sb")
        xch_done, xcl_done, hc_sb = sem("xch_done"), sem("xcl_done"), sem("hc_sb")
        hn_sb, hcT_ps = sem("hn_sb"), sem("hcT_ps")
        kv_ps, kc_sb, vc_sb = sem("kv_ps"), sem("kc_sb"), sem("vc_sb")
        sc_ps, sc_sb, ex_sb, pc_sb = sem("sc_ps"), sem("sc_sb"), sem("ex_sb"), sem("pc_sb")
        pcT_ps, pcT_sb, oc_ps, oc_sb = sem("pcT_ps"), sem("pcT_sb"), sem("oc_ps"), sem("oc_sb")
        s_ps, s_sb, p_sb, pT_ps = sem("s_ps"), sem("s_sb"), sem("p_sb"), sem("pT_ps")
        pT_sbA, pT_sbV, o_ps, o_sb = sem("pT_sbA"), sem("pT_sbV"), sem("o_ps"), sem("o_sb")
        conv_pool, conv_vec = sem("conv_pool"), sem("conv_vec")
        cn_ps, cn_sb, cnT_ps, y2_sb = sem("cn_ps"), sem("cn_sb"), sem("cnT_ps"), sem("y2_sb")
        oT_ps, mh_done, ml_done = sem("oT_ps"), sem("mh_done"), sem("ml_done")
        pss_done = sem("pss_done")
        sg_done, h_done, hT_ps, hh_done, hl_done = (
            sem("sg_done"), sem("h_done"), sem("hT_ps"), sem("hh_done"), sem("hl_done"))
        ws_masked, wsT_ps, wsT_sb, z_sb = sem("ws_masked"), sem("wsT_ps"), sem("wsT_sb"), sem("z_sb")
        z2_done, mixed_ps, gy_done, gyT_ps = sem("z2_done"), sem("mixed_ps"), sem("gy_done"), sem("gyT_ps")
        gh_done, gl_done = sem("gh_done"), sem("gl_done")
        wr_hi, wr_lo, lg_ps, ex_in, ex_out = sem("wr_hi"), sem("wr_lo"), sem("lg_ps"), sem("ex_in"), sem("ex_out")
        m_done, pos_ps, routed = sem("m_done"), sem("pos_ps"), sem("routed")
        sel_done, gath_ps, xgh_done, xgl_done = sem("sel_done"), sem("gath_ps"), sem("xgh_done"), sem("xgl_done")
        pt_ps, pt_sb = sem("pt_ps"), sem("pt_sb")
        msg_done, mh_ok, mhT_ps, mhh_done, mhl_done = (
            sem("msg_done"), sem("mh_ok"), sem("mhT_ps"), sem("mhh_done"), sem("mhl_done"))
        yh_done = [sem(f"yh_done{q}") for q in range(2)]
        comb_ps = [sem(f"comb_ps{k}") for k in range(2 * T)]
        yl_done, acc_done = sem("yl_done"), sem("acc_done")
        act_chain, dve_chain, pool_chain = sem("act_chain"), sem("dve_chain"), sem("pool_chain")

        class Chain:

            def __init__(self, eng, s):
                self.eng, self.sem, self.n, self.more = eng, s, 0, 0

            def link(self, ins):
                ins.then_inc(self.sem, 1)
                self.n += 1
                self.wait()

            def add(self, ins):
                ins.then_inc(self.sem, 1)
                self.n += 1

            def wait(self):
                self.eng.wait_ge(self.sem, self.n + self.more)

        def wait_raw(eng, k, it=0):
            eng.wait_ge(raw_in[raw_slot(k)], raw_count(k) + 16 * unit_dmas(k) * it)

        block = ctx.enter_context(nc.Block())

        @block.sync
        def _(sp):
            sp.dma_start(xres[:, :, :], x[0].rearrange("(t p) d -> p t d", p=P)).then_inc(x_in, 16)
            rows = [(V_MIX, norm_mix_pre.rearrange("l (c p) -> (l c) p", p=P)),
                    (V_FFN, norm_ffn_pre.rearrange("l (c p) -> (l c) p", p=P)),
                    (V_CB, conv_b.rearrange("o (c p) -> (o c) p", p=P)),
                    (V_CG, conv_ln_g.rearrange("o (c p) -> (o c) p", p=P)),
                    (V_CLB, conv_ln_b.rearrange("o (c p) -> (o c) p", p=P)),
                    (V_B1, cmp_b1.rearrange("o k (c p) -> (o k c) p", p=P)),
                    (V_PE, cmp_pe.rearrange("o k (c r) d -> (o k c) (r d)", r=2)),
                    (V_BS, gmlp_b_s.rearrange("o g t -> (o g) t"))]
            assert len(rows) + 3 == VEC_LOADS
            for r, src in rows:
                sp.dma_start(vec_rows[r:r + src.shape[0], :], src).then_inc(vec_in, 16)
            for h in range(2):
                sp.dma_start(vec_rows[V_B2K:V_B2K + 1, h * HD:h * HD + HD], cmp_b2[:, 0, :]).then_inc(vec_in, 16)
            sp.dma_start(cw_rows[0:CC * CONV_W, :],
                         conv_w.rearrange("o w i (c p) -> (o w i c) p", p=P)).then_inc(vec_in, 16)

            def load(k, parts, it=0):
                if k >= RING1:
                    sp.wait_ge(lo_done, k - RING1 + 1 + 9 * it)
                for dst, src in parts:
                    sp.dma_start(dst, src).then_inc(raw_in[raw_slot(k)], 16)

            def slot(k, a):
                return raw[:, raw_slot(k), :].rearrange("p (c n) -> p c n", c=a)

            win = nsa_conv_w_in[0].rearrange("(c p) n -> p c n", p=P)
            g0 = QC + KVC + GATES
            cols = [g0, g0 + CONV_CH, g0 + 256, g0 + CONV_CH + 256, QC, 0, 256, QC + 256, QC + 512]
            for k, c0 in enumerate(cols):
                load(k, [(slot(k, 8), win[:, :, c0:c0 + 256])])
            for j in range(4):
                w1 = cmp_w1[0, j // 2].rearrange("(c p) n -> p c n", p=P)
                load(U_CW1 + j, [(slot(U_CW1 + j, 8), w1[:, 8 * (j % 2):8 * (j % 2) + 8, :])])
            wo = nsa_conv_w_out[0].rearrange("(c p) n -> p c n", p=P)
            for j in range(4):
                load(U_OUT0 + j, [(slot(U_OUT0 + j, 2), wo[:, 2 * j:2 * j + 2, :])])

            fg = ffn_w_gate[0].rearrange("(c p) n -> p c n", p=P)
            fu = ffn_w_up[0].rearrange("(c p) n -> p c n", p=P)
            fd = ffn_w_down[0].rearrange("(c p) n -> p c n", p=P)

            def load_gu(k, half, b, it=0):
                dst = raw[:, raw_slot(k), :].rearrange("p (c u n) -> p c u n", c=4, u=2)
                n0 = b * 256
                load(k, [(dst[:, :, u, :], w[:, 4 * half:4 * half + 4, bass.ds(n0, 256)])
                         for u, w in enumerate((fg, fu))], it)

            def load_down(k, b, it=0):
                load(k, [(slot(k, 2), fd[:, bass.ds(b * 2, 2), :])], it)

            k = U_FFN
            load_gu(k, 0, 0)
            load_gu(k + 1, 1, 0)
            load_gu(k + 2, 0, 1)
            load_gu(k + 3, 1, 1)
            load_down(k + 4, 0)
            with sp.Fori(0, 3) as it:
                for j in range(3):
                    k = U_FFN + 5 + 3 * j
                    b = it * 3 + (FFN_LOOP0 + j)
                    load_gu(k, 0, b, it)
                    load_gu(k + 1, 1, b, it)
                    load_down(k + 2, b - 1, it)
            load_down(U_GM - 1, FFN_BLOCKS - 1)

            gw = gmlp_w_in[0].rearrange("(c p) n -> p c n", p=P)
            for j in range(8):
                cb = (j // 2 + 2) % 4
                load(U_GM + j, [(slot(U_GM + j, 4), gw[:, 4 * (j % 2):4 * (j % 2) + 4, cb * 512:cb * 512 + 512])])
            go = gmlp_w_out[0].rearrange("(c p) n -> p c n", p=P)
            for j in range(4):
                load(U_GMO + j, [(slot(U_GMO + j, 2), go[:, 2 * j:2 * j + 2, :])])

            eg = moe_w_gate[0].rearrange("e (c p) n -> e p c n", p=P)
            eu = moe_w_up[0].rearrange("e (c p) n -> e p c n", p=P)
            ed = moe_w_down[0].rearrange("e (c p) n -> e p c n", p=P)

            def load_pair(it):
                m = 0

                def one(e, w, c0, n, col0, cols):
                    nonlocal m
                    sp.wait_ge(lo_done, U_MOE + m - RING2 + 1 + 2 * MOE_UNITS * it)
                    src = w[bass.ds(e, 1), :, c0:c0 + n, col0:col0 + cols].rearrange("o p c n -> (o p) c n")
                    sp.dma_start(slot(U_MOE + m, n), src).then_inc(raw_in[moe_slot(m)], 16)
                    m += 1

                for j in range(2):
                    e = 2 * it + j
                    for b in range(MOE_BLOCKS):
                        for w in (eu, eg):
                            for half in range(2):
                                one(e, w, 4 * half, 4, b * 512, 512)
                        if b:
                            for half in range(2):
                                one(e, ed, 4 * (b - 1) + 2 * half, 2, 0, D)
                    for half in range(2):
                        one(e, ed, 4 * (MOE_BLOCKS - 1) + 2 * half, 2, 0, D)

            sp.wait_ge(gyT_ps, 4)
            with sp.Fori(0, NE // 2) as it:
                load_pair(it)
            yo = out[0].rearrange("(t p) d -> p t d", p=P)
            for t in range(T):
                sp.wait_ge(x_new, 6 + t + 1)
                sp.dma_start(yo[:, t, :], xres[:, t, :]).then_inc(stored, 16)
            sp.wait_ge(stored, 16 * T)

        @block.gpsimd
        def _(pool):
            g = nc.gpsimd
            g.memset(ident[:, :], 0.0).then_inc(pool_chain, 1)
            g.memset(mask[:, :], 0.0).then_inc(pool_chain, 1)
            g.memset(cadd[:, :, :], 0.0).then_inc(pool_chain, 1)
            g.memset(cmul[:, :, :], 1.0).then_inc(pool_chain, 1)
            g.memset(cT[:, :, 0:CONV_W - 1], 0.0).then_inc(pool_chain, 1)
            g.memset(neg_half[:, :], -0.5).then_inc(pool_chain, 1)
            pool.wait_ge(pool_chain, 6)
            g.affine_select(out=ident[:, :], in_=ident[:, :], compare_op=ALU.not_equal, fill=1.0,
                            base=0, pattern=[[-1, P]], channel_multiplier=1).then_inc(consts, 1)
            g.affine_select(out=mask[:, P:S], in_=mask[:, P:S], compare_op=ALU.is_ge, fill=NEG,
                            base=0, pattern=[[-1, P]], channel_multiplier=1).then_inc(consts, 1)
            for m, fill in ((cadd, NEG), (cmul, 0.0)):
                g.affine_select(out=m[:, :, :], in_=m[:, :, :], compare_op=ALU.is_ge, fill=fill,
                                base=-(CMP_LEN - 1), pattern=[[P, 2], [-CMP_STRIDE, NCMP]],
                                channel_multiplier=1).then_inc(consts, 1)

            pool.wait_ge(consts, 4)
            for g_ in range(2):
                for h in range(2):
                    last = g.tensor_copy(both[:, g_, h * HD:h * HD + HD], ident[:, g_ * HD:g_ * HD + HD])
            last.then_inc(consts, 1)

            rs_n = [0]

            def power(c, w):
                rs_n[0] += 1
                pool.wait_ge(rs_in, rs_n[0])
                g.tensor_tensor(st[:, c:c + w], st[:, c:c + w], neg_half[:, 0:w], ALU.pow).then_inc(rs_out, 1)

            power(2, 2)

            n = 6
            pool.wait_ge(glu_sb, 2)
            pool.wait_ge(vec_sb, 2)
            for cc in (3,):
                w = cw[:, cc:cc + 1]
                g.tensor_scalar(yT[:, cc, :], cT[:, cc, 0:S], w, vec[:, V_CB + cc:V_CB + cc + 1],
                                ALU.mult, ALU.add).then_inc(pool_chain, 1)
                n += 1
                for j in range(1, CONV_W):
                    w = cw[:, j * CC + cc:j * CC + cc + 1]
                    g.tensor_scalar(ptmp, cT[:, cc, j:j + S], w, None, ALU.mult).then_inc(pool_chain, 1)
                    n += 1
                    pool.wait_ge(pool_chain, n)
                    g.tensor_tensor(yT[:, cc, :], yT[:, cc, :], ptmp, ALU.add).then_inc(pool_chain, 1)
                    n += 1
                    pool.wait_ge(pool_chain, n)
            g.tensor_copy(ptmp[:, 0:1], yT[:, 3, 0:1]).then_inc(conv_pool, 1)

            for t in range(T):
                power(71 + 8 * t, 1)
            power(6, 2)
            power(2, 2)
            power(6, 2)
            power(2, 2)

            pool.wait_ge(ws_in, 16)
            g.affine_select(out=ws[:, :, :], in_=ws[:, :, :], compare_op=ALU.is_ge, fill=0.0,
                            base=0, pattern=[[0, 8], [-1, P]], channel_multiplier=1).then_inc(ws_masked, 1)
            for t in range(T):
                power(57, 1)
            pool.wait_ge(gyT_ps, 4)
            g.iota(iota, pattern=[[1, S]], base=0, channel_multiplier=0,
                   allow_small_or_imprecise_dtypes=True).then_inc(route_consts, 1)
            g.memset(ones, 1.0).then_inc(route_consts, 1)
            g.memset(tri, 1.0).then_inc(pool_chain, 1)
            pool.wait_ge(pool_chain, n + 1)
            g.affine_select(out=tri, in_=tri, compare_op=ALU.is_gt, fill=0.0,
                            base=0, pattern=[[1, P]], channel_multiplier=-1).then_inc(route_consts, 1)
            power(6, 2)
            power(2, 2)
            power(6, 2)

        @block.scalar
        def _(act):
            a = nc.scalar
            ch = Chain(act, act_chain)

            def split_hi(k, it=0):
                wait_raw(act, k, it)
                if k >= PARTS:
                    act.wait_ge(unit_used, k - PARTS + 1 + 9 * it)
                a.activation(w_hi[:, k % PARTS, :], raw[:, raw_slot(k), :], ACT.Copy).then_inc(hi_done, 1)

            def moe_hi(m, it):
                act.wait_ge(raw_in[moe_slot(m)], moe_count(m) + 16 * (2 * MOE_UNITS // RING2) * it)
                act.wait_ge(unit_used, U_MOE + m - PARTS + 1 + 2 * MOE_UNITS * it)
                a.activation(w_hi[:, (U_MOE + m) % PARTS, :], raw[:, moe_slot(m), :], ACT.Copy).then_inc(hi_done, 1)

            w2 = cmp_w2[0].rearrange("k (h p) n -> k p h n", p=P)
            for h in range(2):
                act.dma_start(w2k[:, :, h * HD:h * HD + HD], w2[0]).then_inc(small_in, 16)
            act.dma_start(w2v[:, :, :], w2[1]).then_inc(small_in, 16)
            act.dma_start(wgate.rearrange("p (c n) -> p c n", c=KC),
                          nsa_conv_w_in[0].rearrange("(c p) n -> p c n", p=P)[:, :, QC + KVC:QC + KVC + GATES]
                          ).then_inc(small_in, 16)
            act.dma_start(b2v[0:NCMP, :], cmp_b2[0, 1:2, :].partition_broadcast(NCMP)).then_inc(small_in, 16)
            act.dma_start(gpost[:, :], norm_mix_post[0:1, :].partition_broadcast(P)).then_inc(post_in, 16)

            def pre_norm(n):
                for t in range(T):
                    if n == 0:
                        act.wait_ge(x_in, 16)
                    else:
                        act.wait_ge(x_new, 2 * (n - 1) + t + 1)
                    a.activation(xn[:, t, :], xres[:, t, :], ACT.Square,
                                 accum_out=st[:, t:t + 1]).then_inc(ss_done, 1)
                g0 = (V_MIX, V_FFN)[n % 2] + KC * (n // 2)
                if n == 0:
                    act.wait_ge(vec_sb, 1)
                for c in range(KC):
                    if c % 2 == 0:
                        act.wait_ge(xT_ps, 4 * n + c // 2 + 1)
                    ins = a.activation(uT_h[:, c, :], ps[:, c // 2, (c % 2) * S:(c % 2) * S + S], ACT.Copy,
                                       scale=vec[:, g0 + c:g0 + c + 1])
                    if c % 2:
                        ins.then_inc(uh_done, 1)

            def post_norm(n, nxt):
                for t in range(T):
                    if n < 3:
                        a.activation(xn[:, t, :].rearrange("p (h n) -> p h n", h=2), ps[:, 2 * t:2 * t + 2, :],
                                     ACT.Square, accum_out=st[:, 4 + t:5 + t]).then_inc(pss_done, 1)
                    else:
                        a.activation(ra[:, t * D:(t + 1) * D], acc[:, t, :],
                                     ACT.Square, accum_out=st[:, 4 + t:5 + t]).then_inc(pss_done, 1)
                if nxt is not None:
                    act.wait_ge(x_new, 2 * n + 2)
                    act.dma_start(gpost[:, :], nxt.partition_broadcast(P)).then_inc(post_in, 16)

            pre_norm(0)
            act.wait_ge(small_in, 16 * SMALL_LOADS)
            a.activation(ht[:, 0, 0:KC * GATES], wgate, ACT.Copy).then_inc(wg_hi, 1)
            for k in range(4):
                split_hi(k)
            act.wait_ge(unit_used, 2)
            a.activation(yT[:, 0:2, :], ps[:, 5, :].rearrange("p (c t) -> p c t", c=2), ACT.Sigmoid).then_inc(glu_sig, 1)
            split_hi(4)
            split_hi(5)
            act.wait_ge(unit_used, 4)
            a.activation(yT[:, 2:4, :], ps[:, 7, :].rearrange("p (c t) -> p c t", c=2), ACT.Sigmoid).then_inc(glu_sig, 1)
            split_hi(6)
            act.wait_ge(unit_used, U_CMP_IN + 1)
            a.activation(ktmp[:, 0:2, :], ps[:, 2, :].rearrange("p (k t) -> p k t", k=2),
                         ACT.Copy).then_inc(proj_sb, 1)
            split_hi(7)
            for u in range(2):
                act.wait_ge(unit_used, U_Q + u + 1)
                a.activation(qT[:, 2 * u:2 * u + 2, :],
                             ps[:, u, :].rearrange("p (c t) -> p c t", c=2),
                             ACT.Copy, scale=float(HD) ** -0.5).then_inc(proj_sb, 1)
                split_hi(8 + u)
            for u in range(2):
                act.wait_ge(unit_used, U_SLC + u + 1)
                a.activation(ktmp[:, 2 + u, :], ps[:, (3, 7)[u], 0:S], ACT.Copy).then_inc(proj_sb, 1)
                a.activation(vv[u][:, :, :], ps[:, (5, 2)[u], 0:256].rearrange("p (t n) -> p t n", t=T),
                             ACT.Copy).then_inc(proj_sb, 1)
                split_hi(10 + u)
            act.wait_ge(xcmp_sb, 1)
            act.wait_ge(gates_ps, 1)
            a.activation(ra[:, 0:960], probT[:, 0:960], ACT.Copy).then_inc(xch_done, 1)
            act.wait_ge(dup_ps, 2)
            for u in range(2):
                a.activation(kT[u][:, :, :], ps[:, (4, 6)[u], :].rearrange("p (g t) -> p g t", g=2),
                             ACT.Copy).then_inc(proj_sb, 1)
            a.activation(gates[:, :, :], ps[:, 0, 0:T * GATES].rearrange("p (t n) -> p t n", t=T),
                         ACT.Sigmoid).then_inc(proj_sb, 1)
            split_hi(12)
            for kv in range(2):
                act.wait_ge(unit_used, U_CW1 + 2 * kv + 2)
                a.activation(hnat[0:NG, kv, :], ps[0:NG, HIDDEN[kv], 0:CMP_HID], ACT.Copy).then_inc(hn_sb, 1)
                split_hi(13 + kv)
            for kv in range(2):
                act.wait_ge(hcT_ps, kv + 1)
                for h in range(2):
                    b1 = V_B1 + 2 * kv + h
                    a.activation(hc[:, kv, h, :], ps[:, (2, 6)[kv], h * NG:h * NG + NG], ACT.Gelu_apprx_tanh,
                                 bias=vec[:, b1:b1 + 1]).then_inc(hc_sb, 1)
            split_hi(15)
            act.wait_ge(kv_ps, 1)
            a.activation(kcT[:, :], ps[:, 5, 0:NG], ACT.Identity, bias=vec[:, V_B2K:V_B2K + 1]).then_inc(kc_sb, 1)
            act.wait_ge(sc_sb, 1)
            a.activation(prob[:, 0:240], prob[:, 0:240], ACT.Exp).then_inc(ex_sb, 1)
            for b in range(4):
                act.wait_ge(pcT_ps, b + 1)
                a.activation(pcT[0:NCMP, 4 * b:4 * b + 4, :], ps[0:NCMP, 4 + b, :].rearrange("p (q t) -> p q t", q=4),
                             ACT.Copy).then_inc(pcT_sb, 1)
            for t in range(2):
                act.wait_ge(cnT_ps, t + 1)
                for cc in (2 * t, 2 * t + 1):
                    a.activation(y2[:, cc, :], ps[:, 4 + t, (cc % 2) * S:(cc % 2) * S + S], ACT.Silu,
                                 bias=vec[:, V_CLB + cc:V_CLB + cc + 1],
                                 scale=vec[:, V_CG + cc:V_CG + cc + 1]).then_inc(act_chain, 1)
                    ch.n += 1
                ch.wait()
                a.activation(uT_h[:, 4 + 2 * t:6 + 2 * t, :], y2[:, 2 * t:2 * t + 2, :], ACT.Copy).then_inc(mh_done, 1)
            for m in range(8):
                nk = P * (m % 2 + 1)
                pr = prob[:, (m % 2) * 1024:(m % 2) * 1024 + 4 * nk].rearrange("p (h k) -> p h k", h=4)
                act.wait_ge(s_sb, m + 1)
                for h in range(4):
                    ins = a.activation(pr[:, h, :], pr[:, h, :], ACT.Exp, bias=st[:, 16 + 4 * (m % 2) + h:17 + 4 * (m % 2) + h],
                                       accum_out=st[:, 24 + 4 * (m % 2) + h:25 + 4 * (m % 2) + h])
                ins.then_inc(p_sb, 1)
                act.wait_ge(pT_ps, m + 1)
                a.activation(probT[:, 0:512], ps[:, 4, :], ACT.Copy).then_inc(pT_sbA, 1)
            for b in range(2):
                act.wait_ge(oT_ps, b + 1)
                a.activation(uT_h[:, 2 * b:2 * b + 2, :], ps[:, 4 + b, :].rearrange("p (c t) -> p c t", c=2),
                             ACT.Copy).then_inc(mh_done, 1)
            split_hi(16)
            act.wait_ge(unit_used, U_FFN)
            post_norm(0, norm_ffn_post[0:1, :])

            pre_norm(1)
            split_hi(17)
            split_hi(18)

            def ffn_silu(b):
                for t in range(T):
                    a.activation(sg[:, t * 256:t * 256 + 256], ps[:, 4 + t, 0:256], ACT.Silu).then_inc(sg_done, 1)

            def ffn_hT(b):
                act.wait_ge(hT_ps, b + 1)
                a.activation(ht[:, 0, 0:512], ps[:, 6, :], ACT.Copy).then_inc(hh_done, 1)

            split_hi(19)
            split_hi(20)
            act.wait_ge(unit_used, 19)
            ffn_silu(0)
            ffn_hT(0)

            def ffn_block(b, k0, it=0):
                split_hi(k0 + 2, it)
                split_hi(k0 + 3, it)
                act.wait_ge(unit_used, k0 + 2 + 9 * it)
                ffn_silu(b)
                split_hi(k0 + 4, it)
                ffn_hT(b)

            ffn_block(1, 19)
            with act.Fori(0, 2) as it:
                for j in range(3):
                    ffn_block(it * 3 + (2 + j), U_FFN + 5 + 3 * j, it)
            for b in range(8, FFN_BLOCKS):
                ffn_block(b, 16 + 3 * b)
            act.wait_ge(unit_used, U_GM)
            post_norm(1, norm_mix_post[1:2, :])
            act.dma_start(ws[:, :, :], gmlp_w_s[0].rearrange("g t s -> t g s")).then_inc(ws_in, 16)
            act.dma_start(ln_g, gmlp_ln_g.partition_broadcast(P)).then_inc(gm_in, 16)
            act.dma_start(ln_b, gmlp_ln_b.partition_broadcast(P)).then_inc(gm_in, 16)

            pre_norm(2)
            for b in range(2):
                act.wait_ge(wsT_ps, b + 1)
                a.activation(wsT[:, 4 * b:4 * b + 4, :], ps[:, b, :].rearrange("p (g t) -> p g t", g=4),
                             ACT.Copy).then_inc(wsT_sb, 1)
            split_hi(51)
            split_hi(52)
            for cb in range(4):
                k = U_GM + 2 * cb
                split_hi(k + 3)
                act.wait_ge(unit_used, k + 2)
                z = z2 if cb < 2 else z1
                for t in range(T):
                    a.activation(z[:, t, (cb % 2) * 512:(cb % 2) * 512 + 512], ps[:, 4 + 2 * (cb % 2) + t, :],
                                 ACT.Gelu_apprx_tanh).then_inc(z_sb, 1)
                if cb < 3:
                    split_hi(k + 4)
            for b in range(4):
                act.wait_ge(gyT_ps, b + 1)
                a.activation(uT_h[:, 2 * b:2 * b + 2, :], ps[:, 4 + b, :].rearrange("p (c t) -> p c t", c=2),
                             ACT.Copy).then_inc(gh_done, 1)
            split_hi(60)
            split_hi(61)
            act.wait_ge(unit_used, U_MOE)
            post_norm(2, None)

            act.wait_ge(x_new, 6)
            act.dma_start(router, moe_w_router[0].rearrange("(c p) e -> p c e", p=P)).then_inc(router_in, 16)
            pre_norm(3)
            act.wait_ge(router_in, 16)
            a.activation(ht[:, 0, 0:KC * NE], gpost[:, 512:576], ACT.Copy).then_inc(wr_hi, 1)
            act.wait_ge(ex_in, 1)
            a.activation(st[:, 42:44], st[:, 40:42], ACT.Exp).then_inc(ex_out, 1)

            def y_hi(e, nt):
                act.wait_ge(unit_used, U_MOE + MOE_UNITS * (e + 1))
                for i in range(nt):
                    for q in range(2):
                        ins = a.activation(y_part(0, i, q), ps[:, 2 * i + q, :], ACT.Copy)
                        if i == nt - 1:
                            ins.then_inc(yh_done[q], 1)

            def gather_hi(e, nt):
                gf = V_FFN + KC
                act.wait_ge(gath_ps, e + 1)
                if nt == 2:
                    act.wait_ge(comb_ps[3], e)
                w = nt * P
                for c in range(KC):
                    bank, o = 4 + c * w // 512, c * w % 512
                    ins = a.activation(ra[:, c * w:c * w + w], ps[:, bank, o:o + w], ACT.Copy,
                                       scale=vec[:, gf + c:gf + c + 1])
                    if c % 4 == 3:
                        ins.then_inc(xgh_done, 1)

            def blocks(e, j, it, nt):
                act.wait_ge(pt_ps, e + 1)
                a.activation(pt01[:, 0:nt, :], ps[:, 4, 0:nt * S].rearrange("p (i t) -> p i t", i=nt),
                             ACT.Copy).then_inc(pt_sb, 1)
                m0 = MOE_UNITS * j

                def silu(b):
                    g_b = 3 if b == 0 else 6 * b + 1
                    act.wait_ge(unit_used, U_MOE + g_b + 1 + MOE_UNITS * e)
                    for i in range(nt):
                        ins = a.activation(esg[:, i, :], ps[:, 4 + 2 * i, :], ACT.Silu)
                    ins.then_inc(msg_done, 1)

                def hT(b):
                    act.wait_ge(mhT_ps, MOE_BLOCKS * e + (b + 1))
                    for i in range(nt):
                        ins = a.activation(ht[:, 0, 512 * i:512 * i + 512], ps[:, 4 + 2 * i, :], ACT.Copy)
                    ins.then_inc(mhh_done, 1)

                for m in range(3, 6):
                    moe_hi(m0 + m, it)
                silu(0)
                hT(0)
                for b in range(1, MOE_BLOCKS):
                    k = 4 + 6 * (b - 1)
                    for m in range(k + 2, k + 6):
                        moe_hi(m0 + m, it)
                    silu(b)
                    moe_hi(m0 + k + 6, it)
                    moe_hi(m0 + k + 7, it)
                    hT(b)

            act.wait_ge(routed, 1)
            with act.Fori(0, NE // 2) as it:
                for j in range(2):
                    e = 2 * it + j
                    moe_hi(MOE_UNITS * j, it)
                    moe_hi(MOE_UNITS * j + 1, it)
                    last = act.value_load(flag[0:1, bass.ds(e + NE, 1)], min_val=0, max_val=2)
                    for nt in (1, 2):
                        with act.If(last == nt):
                            y_hi(e - 1, nt)
                    two = act.value_load(flag[0:1, bass.ds(e, 1)], min_val=0, max_val=1)
                    for nt in (1, 2):
                        with act.If(two == nt - 1):
                            gather_hi(e, nt)
                            moe_hi(MOE_UNITS * j + 2, it)
                            blocks(e, j, it, nt)
            last = act.value_load(flag[0:1, 2 * NE:2 * NE + 1], min_val=0, max_val=2)
            for nt in (1, 2):
                with act.If(last == nt):
                    y_hi(NE - 1, nt)
            act.wait_ge(ex_in, 2)
            act.dma_start(gpost[:, :], norm_ffn_post[1:2, :].partition_broadcast(P)).then_inc(post_in, 16)
            post_norm(3, None)

        @block.vector
        def _(dve):
            v = nc.vector
            ch = Chain(dve, dve_chain)
            link = ch.link
            rs_n = [0]

            def split_lo(k, it=0):
                dve.wait_ge(hi_done, k + 1 + 9 * it)
                v.tensor_tensor(w_lo[:, k % PARTS, :], raw[:, raw_slot(k), :],
                                w_hi[:, k % PARTS, :].bitcast(F32), ALU.subtract).then_inc(lo_done, 1)

            def moe_lo(m, it):
                dve.wait_ge(hi_done, U_MOE + m + 1 + 2 * MOE_UNITS * it)
                s = (U_MOE + m) % PARTS
                v.tensor_tensor(w_lo[:, s, :], raw[:, moe_slot(m), :], w_hi[:, s, :].bitcast(F32),
                                ALU.subtract).then_inc(lo_done, 1)

            def rsqrt(dst, src, scale):
                v.tensor_scalar(dst, src, scale, EPS, ALU.mult, ALU.add).then_inc(rs_in, 1)
                rs_n[0] += 1
                dve.wait_ge(rs_out, rs_n[0])

            def pre_norm(n):
                dve.wait_ge(ss_done, 2 * n + 2)
                rsqrt(st[:, 2:4], st[:, 0:2], 1.0 / D)
                for t in range(T):
                    v.tensor_scalar(xn[:, t, :], xres[:, t, :], st[:, 2 + t:3 + t], None, ALU.mult).then_inc(xn_done, 1)
                g0 = (V_MIX, V_FFN)[n % 2] + KC * (n // 2)
                for c in range(KC):
                    if c % 2 == 0:
                        dve.wait_ge(uh_done, 4 * n + c // 2 + 1)
                    ins = v.scalar_tensor_tensor(out=uT_l[:, c, :], in0=ps[:, c // 2, (c % 2) * S:(c % 2) * S + S],
                                                 scalar=vec[:, g0 + c:g0 + c + 1], in1=uT_h[:, c, :].bitcast(F32),
                                                 op0=ALU.mult, op1=ALU.subtract)
                    if c % 2:
                        ins.then_inc(ul_done, 1)

            def post_norm(n):
                dve.wait_ge(pss_done, 2 * n + 2)
                rsqrt(st[:, 6:8], st[:, 4:6], 1.0 / D)
                dve.wait_ge(post_in, 16 * (n + 1))
                for t in range(T):
                    if n < 3:
                        src = ps[:, 2 * t:2 * t + 2, :]
                        dst = xn[:, t, :].rearrange("p (h n) -> p h n", h=2)
                        g = gpost[:, :].rearrange("p (h n) -> p h n", h=2)
                    else:
                        src, dst, g = acc[:, t, :], xn[:, t, :], gpost[:, :]
                    link(v.scalar_tensor_tensor(out=dst, in0=src, scalar=st[:, 6 + t:7 + t],
                                                in1=g, op0=ALU.mult, op1=ALU.mult))
                    v.tensor_tensor(xres[:, t, :], xres[:, t, :], xn[:, t, :], ALU.add).then_inc(x_new, 1)

            dve.wait_ge(vec_ps, 1)
            v.tensor_copy(vec[:, :], ps[:, 7, 0:V_ROWS]).then_inc(vec_sb, 1)
            v.tensor_copy(cw, ps[:, 7, P:P + CC * CONV_W]).then_inc(vec_sb, 1)
            pre_norm(0)
            dve.wait_ge(wg_hi, 1)
            v.tensor_tensor(ht[:, 1, 0:KC * GATES], wgate, ht[:, 0, 0:KC * GATES].bitcast(F32),
                            ALU.subtract).then_inc(wg_lo, 1)
            def glu(i):
                dve.wait_ge(glu_sig, i + 1)
                v.tensor_tensor(cT[:, 2 * i:2 * i + 2, CONV_W - 1:PADT],
                                ps[:, (4, 6)[i], :].rearrange("p (c t) -> p c t", c=2),
                                yT[:, 2 * i:2 * i + 2, :], ALU.mult).then_inc(glu_sb, 1)

            def conv_steps(lo, hi):
                for s_ in range(lo, hi):
                    ch.wait()
                    if s_ == 0 or s_ == LATE:
                        dve.wait_ge(glu_sb, 1 if s_ == 0 else 2)
                    for cc, j in ((0, s_), (1, s_), (2, s_ - LATE)):
                        if not 0 <= j < CONV_W:
                            continue
                        w = cw[:, j * CC + cc:j * CC + cc + 1]
                        if j == 0:
                            ins = v.tensor_scalar(yT[:, cc, :], cT[:, cc, 0:S], w,
                                                  vec[:, V_CB + cc:V_CB + cc + 1], ALU.mult, ALU.add)
                        else:
                            ins = v.scalar_tensor_tensor(out=yT[:, cc, :], in0=cT[:, cc, j:j + S], scalar=w,
                                                         in1=yT[:, cc, :], op0=ALU.mult, op1=ALU.add)
                        ch.add(ins)

            def compressor_input():
                dve.wait_ge(dup_ps, 1)
                for kv in range(2):
                    for g in range(2):
                        for r in range(2):
                            pr = slice(HD * r, HD * r + HD)
                            src = ps[pr, (4, 6)[kv], g * S:g * S + S].rearrange("p (m i) -> p m i", i=CMP_STRIDE)
                            for h in range(2):
                                dst = xcmp[pr, kv, 8 * h:8 * h + 8, g, :]
                                pe = vec[pr, V_PE + 16 * kv + 8 * h:V_PE + 16 * kv + 8 * h + 8]
                                last = v.tensor_tensor(
                                    dst, src[:, h:h + NCMP, r:CMP_STRIDE:2].rearrange("p n c -> p c n"),
                                    pe.unsqueeze(2).to_broadcast([HD, 8, NCMP]), ALU.add)
                last.then_inc(xcmp_sb, 1)

            LATE = 8
            for k in range(5):
                split_lo(k)
            glu(0)
            split_lo(5)
            conv_steps(0, 4)
            split_lo(6)
            glu(1)
            conv_steps(4, 6)
            split_lo(7)
            conv_steps(6, 9)
            split_lo(8)
            compressor_input()
            split_lo(9)
            conv_steps(9, 12)
            split_lo(10)
            conv_steps(12, 15)
            split_lo(11)
            dve.wait_ge(xch_done, 1)
            v.tensor_tensor(ra[:, 1024:1984], probT[:, 0:960], ra[:, 0:960].bitcast(F32),
                            ALU.subtract).then_inc(xcl_done, 1)
            conv_steps(15, 18)
            split_lo(12)
            conv_steps(18, 21)
            split_lo(13)
            conv_steps(21, 24)
            split_lo(14)
            conv_steps(24, CONV_W + LATE)
            ch.wait()
            v.tensor_copy(st[:, 61:62], yT[:, 2, 0:1]).then_inc(conv_vec, 1)
            dve.wait_ge(kv_ps, 2)
            v.tensor_tensor(vc[0:NCMP, :, :], ps[0:NCMP, 4, 0:2 * HD].rearrange("p (g d) -> p g d", g=2),
                            b2v[0:NCMP, :].unsqueeze(1).to_broadcast([NCMP, 2, HD]), ALU.add).then_inc(vc_sb, 1)
            split_lo(15)

            pc = prob[:, 0:240].rearrange("p (f i q n) -> p f i q n", f=2, i=2, q=4)
            dve.wait_ge(sc_ps, 1)
            dve.wait_ge(consts, 4)
            for i in range(2):
                ch.add(v.tensor_tensor(pc[:, :, i, :, :],
                                       ps[:, 0:2, i * 60:i * 60 + 60].rearrange("p f (q n) -> p f q n", q=4),
                                       cadd[:, i, :].unsqueeze(1).unsqueeze(1).to_broadcast([P, 2, 4, NCMP]), ALU.add))
            ch.wait()
            pq = prob[:, 0:240].rearrange("p (q n) -> p q n", n=NCMP)
            link(v.tensor_reduce(st[:, 44:60], pq, AX.X, ALU.max))
            v.tensor_tensor(pq, pq, st[:, 44:60].unsqueeze(2).to_broadcast([P, 16, NCMP]),
                            ALU.subtract).then_inc(sc_sb, 1)
            dve.wait_ge(ex_sb, 1)
            link(v.tensor_reduce(st[:, 44:60], pq, AX.X, ALU.add))
            link(v.reciprocal(st[:, 44:60], st[:, 44:60]))
            coef = st[:, 44:60].rearrange("p (f i q) -> p f i q", f=2, i=2)
            dve.wait_ge(proj_sb, 8)
            for i in range(2):
                for f in range(2):
                    gv = gates[:, i, :].rearrange("p (q f k) -> p q f k", q=4, f=2)[:, :, f, 0]
                    ch.add(v.tensor_tensor(coef[:, f, i, :], coef[:, f, i, :], gv, ALU.mult))
                last = v.tensor_tensor(pc[:, :, i, :, :], pc[:, :, i, :, :],
                                       cmul[:, i, :].unsqueeze(1).unsqueeze(1).to_broadcast([P, 2, 4, NCMP]), ALU.mult)
                ch.add(last)
            ch.wait()
            v.tensor_copy(atmp[:, 0:240], prob[:, 0:240]).then_inc(pc_sb, 1)
            for t in range(T):
                o = 64 + 8 * t
                dve.wait_ge(cn_ps, t + 1)
                link(v.bn_stats(st[:, o:o + 6], ps[:, 2 + t, :]))
                link(v.bn_aggr(st[:, o + 6:o + 8], st[:, o:o + 6]))
                rsqrt(st[:, o + 7:o + 8], st[:, o + 7:o + 8], 1.0)
                v.tensor_scalar(cn[:, t, :], ps[:, 2 + t, :], st[:, o + 6:o + 7], st[:, o + 7:o + 8],
                                ALU.subtract, ALU.mult).then_inc(cn_sb, 1)
            for i in range(2):
                dve.wait_ge(oc_ps, i + 1)
                v.tensor_tensor(oacc[:, i, :].rearrange("p (q f d) -> p q f d", q=4, f=2),
                                ps[:, i, :].rearrange("p (q f d) -> p q f d", q=4, f=2),
                                coef[:, :, i, :].rearrange("p f q -> p q f").unsqueeze(3).to_broadcast([P, 4, 2, HD]),
                                ALU.mult).then_inc(oc_sb, 1)

            for t in range(2):
                dve.wait_ge(mh_done, t + 1)
                v.tensor_tensor(uT_l[:, 4 + 2 * t:6 + 2 * t, :], y2[:, 2 * t:2 * t + 2, :],
                                uT_h[:, 4 + 2 * t:6 + 2 * t, :].bitcast(F32), ALU.subtract).then_inc(ml_done, 1)

            def att_scores(m):
                i = m % 2
                nk = P * (i + 1)
                pr = prob[:, i * 1024:i * 1024 + 4 * nk]
                mx = st[:, 16 + 4 * i:20 + 4 * i]
                dve.wait_ge(s_ps, m + 1)
                if m < 2:
                    dve.wait_ge(oc_ps, 2)
                link(v.tensor_tensor(pr.rearrange("p (f j k) -> p f j k", f=2, j=2),
                                     ps[:, 2 * i:2 * i + 2, 0:2 * nk].rearrange("p f (j k) -> p f j k", j=2),
                                     mask[:, S - nk:S].unsqueeze(1).unsqueeze(1).to_broadcast([P, 2, 2, nk]), ALU.add))
                link(v.tensor_reduce(mx, pr.rearrange("p (h k) -> p h k", h=4), AX.X, ALU.max))
                v.tensor_scalar(mx, mx, -1.0, None, ALU.mult).then_inc(s_sb, 1)

            def att_out(m):
                br, g, i = m // 4, m // 2 % 2, m % 2
                if i:
                    dve.wait_ge(pT_ps, m + 1)
                    v.tensor_copy(probT[:, 512:1024], ps[:, 5, :]).then_inc(pT_sbV, 1)
                dve.wait_ge(p_sb, m + 1)
                cf = st[:, 32 + 4 * i:36 + 4 * i]
                link(v.reciprocal(cf, st[:, 24 + 4 * i:28 + 4 * i]))
                gv = gates[:, i, 12 * g:12 * g + 12].rearrange("p (j f k) -> p f j k", j=2, f=2)[:, :, :, 1 + br]
                link(v.tensor_tensor(cf.rearrange("p (f j) -> p f j", f=2), cf.rearrange("p (f j) -> p f j", f=2),
                                     gv, ALU.mult))
                dve.wait_ge(o_ps, m + 1)
                link(v.tensor_tensor(atmp.rearrange("p (j f d) -> p j f d", j=2, f=2),
                                     ps[:, 6 + i, 0:256].rearrange("p (j f d) -> p j f d", j=2, f=2),
                                     cf.rearrange("p (f j) -> p j f", f=2).unsqueeze(3).to_broadcast([P, 2, 2, HD]),
                                     ALU.mult))
                link(v.tensor_tensor(oacc[:, i, g * 256:g * 256 + 256], oacc[:, i, g * 256:g * 256 + 256],
                                     atmp, ALU.add))
                v.tensor_copy(st[:, 60:61], cf[:, 0:1]).then_inc(o_sb, 1)

            att_scores(0)
            for m in range(8):
                if m < 7:
                    att_scores(m + 1)
                att_out(m)

            for b in range(2):
                dve.wait_ge(mh_done, 3 + b)
                v.tensor_tensor(uT_l[:, 2 * b:2 * b + 2, :], ps[:, 4 + b, :].rearrange("p (c t) -> p c t", c=2),
                                uT_h[:, 2 * b:2 * b + 2, :].bitcast(F32), ALU.subtract).then_inc(ml_done, 1)
            split_lo(16)
            post_norm(0)

            pre_norm(1)

            def ffn_h(b):
                for t in range(T):
                    dve.wait_ge(sg_done, 2 * b + (t + 1))
                    v.tensor_tensor(hbuf[:, t * 256:t * 256 + 256], sg[:, t * 256:t * 256 + 256],
                                    ps[:, 4 + t, 256:512], ALU.mult).then_inc(h_done, 1)

            def ffn_hT(b):
                dve.wait_ge(hh_done, b + 1)
                v.tensor_tensor(ht[:, 1, 0:512], ps[:, 6, :], ht[:, 0, 0:512].bitcast(F32), ALU.subtract).then_inc(hl_done, 1)

            def ffn_block(b, k0, it=0):
                split_lo(k0 + 2, it)
                split_lo(k0 + 3, it)
                ffn_h(b)
                split_lo(k0 + 4, it)
                ffn_hT(b)

            for k in range(17, 21):
                split_lo(k)
            ffn_h(0)
            ffn_hT(0)
            ffn_block(1, 19)
            with dve.Fori(0, 2) as it:
                for j in range(3):
                    ffn_block(it * 3 + (2 + j), U_FFN + 5 + 3 * j, it)
            for b in range(8, FFN_BLOCKS):
                ffn_block(b, 16 + 3 * b)
            post_norm(1)

            pre_norm(2)
            split_lo(51)
            split_lo(52)
            for cb in range(4):
                k = U_GM + 2 * cb
                split_lo(k + 3)
                if cb < 3:
                    split_lo(k + 4)
                if cb == 1:
                    dve.wait_ge(gm_in, 32)
                    dve.wait_ge(z_sb, 4)
                    for t in range(T):
                        for h in range(2):
                            ch.add(v.bn_stats(st[:, 44 + 6 * h:50 + 6 * h], z2[:, t, h * 512:h * 512 + 512]))
                        ch.wait()
                        link(v.bn_aggr(st[:, 56:58], st[:, 44:56].rearrange("p (h s) -> p h s", h=2)))
                        rsqrt(st[:, 57:58], st[:, 57:58], 1.0)
                        link(v.tensor_scalar(z2[:, t, :], z2[:, t, :], st[:, 56:57], st[:, 57:58],
                                             ALU.subtract, ALU.mult))
                        link(v.tensor_tensor(z2[:, t, :], z2[:, t, :], ln_g, ALU.mult))
                        v.tensor_tensor(z2[:, t, :], z2[:, t, :], ln_b, ALU.add).then_inc(z2_done, 1)
            for t in range(T):
                for h in range(2):
                    dve.wait_ge(mixed_ps, 2 * t + h + 1)
                    dve.wait_ge(z_sb, 8)
                    for g in range(4 * h, 4 * h + 4):
                        last = v.scalar_tensor_tensor(
                            out=z1[:, t, g * P:g * P + P], in0=ps[:, 2 * t + h, (g % 4) * P:(g % 4) * P + P],
                            scalar=vec[:, V_BS + g:V_BS + g + 1], in1=z1[:, t, g * P:g * P + P],
                            op0=ALU.add, op1=ALU.mult)
                    last.then_inc(gy_done, 1)
            for b in range(4):
                dve.wait_ge(gh_done, b + 1)
                v.tensor_tensor(uT_l[:, 2 * b:2 * b + 2, :], ps[:, 4 + b, :].rearrange("p (c t) -> p c t", c=2),
                                uT_h[:, 2 * b:2 * b + 2, :].bitcast(F32), ALU.subtract).then_inc(gl_done, 1)
            split_lo(60)
            split_lo(61)
            post_norm(2)

            pre_norm(3)
            dve.wait_ge(wr_hi, 1)
            v.tensor_tensor(ht[:, 1, 0:KC * NE], gpost[:, 512:576], ht[:, 0, 0:KC * NE].bitcast(F32),
                            ALU.subtract).then_inc(wr_lo, 1)

            def small(i):
                return rt[:, 16 * i:16 * i + 16].rearrange("p (t e) -> p t e", t=T)

            lg, eq, mk1, mk2, io8, mm, _, mr, pos, cnt = (small(i) for i in range(10))
            col = rt[:, 160:176]
            w_out = rt[:, 192:210].rearrange("p (t e) -> p t e", t=T)

            def over(c):
                return c.unsqueeze(2).to_broadcast([P, T, NE])

            dve.wait_ge(route_consts, 3)
            link(v.tensor_scalar(io8, iota[:, 0:NE].unsqueeze(1).to_broadcast([P, T, NE]), float(-NE), None, ALU.add))
            dve.wait_ge(lg_ps, 1)
            link(v.tensor_copy(lg, ps[:, 4, 0:T * NE].rearrange("p (t e) -> p t e", t=T)))

            def top(mx, idx, mk):
                link(v.tensor_reduce(mx, lg, AX.X, ALU.max))
                link(v.tensor_tensor(eq, lg, over(mx), ALU.is_equal))
                link(v.tensor_tensor(eq, eq, io8, ALU.mult))
                link(v.tensor_reduce(idx, eq, AX.X, ALU.min))
                link(v.tensor_tensor(mk, io8, over(idx), ALU.is_equal))

            top(col[:, 0:2], col[:, 4:6], mk1)
            link(v.scalar_tensor_tensor(out=lg, in0=mk1, scalar=-3e38, in1=lg, op0=ALU.mult, op1=ALU.add))
            top(col[:, 2:4], col[:, 4:6], mk2)
            v.tensor_tensor(st[:, 40:42], col[:, 2:4], col[:, 0:2], ALU.subtract).then_inc(ex_in, 1)
            link(v.tensor_tensor(mm, mk1, mk2, ALU.add))
            link(v.tensor_tensor(mr, mm, over(st[:, 2:4]), ALU.mult))
            v.tensor_copy(eq, mm).then_inc(m_done, 1)
            dve.wait_ge(ex_out, 1)
            link(v.tensor_scalar(col[:, 0:2], st[:, 42:44], 1.0, None, ALU.add))
            link(v.reciprocal(col[:, 0:2], col[:, 0:2]))
            link(v.tensor_tensor(col[:, 2:4], col[:, 0:2], st[:, 42:44], ALU.mult))
            link(v.tensor_tensor(mk1, mk1, over(col[:, 0:2]), ALU.mult))
            link(v.tensor_tensor(mk2, mk2, over(col[:, 2:4]), ALU.mult))
            link(v.memset(w_out, 0.0))
            link(v.tensor_tensor(w_out[:, :, 1:NE + 1], mk1, mk2, ALU.add))
            dve.wait_ge(pos_ps, 1)
            link(v.tensor_copy(pos, ps[:, 5, 0:T * NE].rearrange("p (t e) -> p t e", t=T)))
            two, last = cnt[:, 0, :], rt[:, 176:176 + NE + 1]
            link(v.tensor_scalar(two, ps[:, 5, T * NE:(T + 1) * NE], float(ONE_TILE), None, ALU.is_gt))
            link(v.memset(last, 0.0))
            link(v.tensor_scalar(last[:, 1:NE + 1], two, 1.0, None, ALU.add))
            link(v.tensor_copy(flag[:, 0:NE], two))
            v.tensor_copy(flag[:, NE:2 * NE + 1], last).then_inc(routed, 1)
            link(v.memset(acc[:, :, :], 0.0))

            def select(e, nt):
                for dst, m in ((selr, mr), (sel01, mm)):
                    for t in range(T):
                        ins = v.tensor_scalar(dst[:, t, 0:nt * P], iota[:, 0:nt * P], pos[:, t, bass.ds(e, 1)],
                                              m[:, t, bass.ds(e, 1)], ALU.is_equal, ALU.mult)
                ins.then_inc(sel_done, 1)

            def y_lo(e, nt):
                for i in range(nt):
                    for q in range(2):
                        if i == 0:
                            dve.wait_ge(yh_done[q], e + 1)
                        ins = v.tensor_tensor(y_part(1, i, q), ps[:, 2 * i + q, :],
                                              y_part(0, i, q).bitcast(F32), ALU.subtract)
                        if i == nt - 1:
                            ins.then_inc(yl_done, 1)

            def gather_lo(e, nt):
                gf, w = V_FFN + KC, nt * P
                for c in range(KC):
                    if c % 4 == 0:
                        dve.wait_ge(xgh_done, 2 * e + (c // 4 + 1))
                    bank, o = 4 + c * w // 512, c * w % 512
                    ins = v.scalar_tensor_tensor(
                        out=ra[:, 2048 + c * w:2048 + c * w + w], in0=ps[:, bank, o:o + w],
                        scalar=vec[:, gf + c:gf + c + 1], in1=ra[:, c * w:c * w + w].bitcast(F32),
                        op0=ALU.mult, op1=ALU.subtract)
                ins.then_inc(xgl_done, 1)

            def add_out(e):
                for t in range(T):
                    for q in range(2):
                        dve.wait_ge(comb_ps[2 * t + q], e + 1)
                        a_ = acc[:, t, q * 512:q * 512 + 512]
                        v.scalar_tensor_tensor(out=a_, in0=ps[:, (2, 0)[t] + q, :], scalar=w_out[:, t, bass.ds(e + 1, 1)],
                                               in1=a_, op0=ALU.mult, op1=ALU.add).then_inc(acc_done, 1)

            def blocks(e, j, it, nt):
                m0 = MOE_UNITS * j

                def h(b):
                    dve.wait_ge(msg_done, MOE_BLOCKS * e + (b + 1))
                    for i in range(nt):
                        ins = v.tensor_tensor(eh[:, i, :], esg[:, i, :], ps[:, 5 + 2 * i, :], ALU.mult)
                    ins.then_inc(mh_ok, 1)

                def hT(b):
                    dve.wait_ge(mhh_done, MOE_BLOCKS * e + (b + 1))
                    for i in range(nt):
                        ins = v.tensor_tensor(ht[:, 1, 512 * i:512 * i + 512], ps[:, 4 + 2 * i, :],
                                              ht[:, 0, 512 * i:512 * i + 512].bitcast(F32), ALU.subtract)
                    ins.then_inc(mhl_done, 1)

                dve.wait_ge(acc_done, 4 * e)
                for m in range(3, 6):
                    moe_lo(m0 + m, it)
                h(0)
                hT(0)
                for b in range(1, MOE_BLOCKS):
                    k = 4 + 6 * (b - 1)
                    for m in range(k + 2, k + 6):
                        moe_lo(m0 + m, it)
                    h(b)
                    moe_lo(m0 + k + 6, it)
                    moe_lo(m0 + k + 7, it)
                    hT(b)

            with dve.Fori(0, NE // 2) as it:
                for j in range(2):
                    e = 2 * it + j
                    two_e = dve.value_load(flag[0:1, bass.ds(e, 1)], min_val=0, max_val=1)
                    last_e = dve.value_load(flag[0:1, bass.ds(e + NE, 1)], min_val=0, max_val=2)
                    for nt in (1, 2):
                        with dve.If(two_e == nt - 1):
                            select(e, nt)
                    moe_lo(MOE_UNITS * j, it)
                    moe_lo(MOE_UNITS * j + 1, it)
                    for nt in (1, 2):
                        with dve.If(last_e == nt):
                            y_lo(e - 1, nt)
                    for nt in (1, 2):
                        with dve.If(two_e == nt - 1):
                            gather_lo(e, nt)
                    moe_lo(MOE_UNITS * j + 2, it)
                    with dve.If(last_e > 0):
                        add_out(e - 1)
                    for nt in (1, 2):
                        with dve.If(two_e == nt - 1):
                            blocks(e, j, it, nt)
            last_e = dve.value_load(flag[0:1, 2 * NE:2 * NE + 1], min_val=0, max_val=2)
            for nt in (1, 2):
                with dve.If(last_e == nt):
                    y_lo(NE - 1, nt)
            add_out(NE - 1)
            dve.wait_ge(acc_done, 4 * NE)
            v.tensor_copy(st[:, 62:63], acc[:, 0, 0:1]).then_inc(ex_in, 1)
            post_norm(3)

        @block.tensor
        def _(pe):
            t_ = nc.tensor

            def mm3(dst, lh, ll, rh, rl, start, stop):
                t_.matmul(dst, lh, rh, start=start, stop=False)
                t_.matmul(dst, lh, rl, start=False, stop=False)
                return t_.matmul(dst, ll, rh, start=False, stop=stop)

            def unit(k, it=0):
                pe.wait_ge(lo_done, k + 1 + 9 * it)
                return w_hi[:, k % PARTS, :], w_lo[:, k % PARTS, :]

            def views(k, c, it=0):
                h, l = unit(k, it)
                return (h.rearrange("p (c n) -> p c n", c=c), l.rearrange("p (c n) -> p c n", c=c))

            def pre_norm(n):
                for c in range(KC):
                    for t in range(T):
                        if c == 0:
                            pe.wait_ge(xn_done, 2 * n + 2)
                        last = t_.transpose(ps[:, c // 2, (c % 2) * S + t * P:(c % 2) * S + t * P + P],
                                            xn[:, t, c * P:c * P + P], ident[:, :])
                    if c % 2:
                        last.then_inc(xT_ps, 1)

            def out_proj(k0, lhs_ready):
                for j in range(4):
                    h, l = views(k0 + j, 2)
                    for kk in range(2):
                        c = 2 * j + kk
                        for t in range(T):
                            for q in range(2):
                                last = mm3(ps[:, 2 * t + q, :], uT_h[:, c, t * P:t * P + P], uT_l[:, c, t * P:t * P + P],
                                           h[:, kk, q * 512:q * 512 + 512], l[:, kk, q * 512:q * 512 + 512],
                                           c == 0, c == KC - 1)
                    last.then_inc(unit_used, 1)

            pe.wait_ge(consts, 1)
            pe.wait_ge(vec_in, 16 * VEC_LOADS)
            t_.transpose(ps[:, 7, 0:V_ROWS], vec_rows[0:V_ROWS, :], ident[0:V_ROWS, 0:V_ROWS])
            t_.transpose(ps[:, 7, P:P + CC * CONV_W], cw_rows[0:CC * CONV_W, :],
                         ident[0:CC * CONV_W, 0:CC * CONV_W]).then_inc(vec_ps, 1)
            pre_norm(0)
            pe.wait_ge(ul_done, 4)

            def cols_proj(dst, h, l, c0):
                for c in range(KC):
                    last = mm3(dst, h[:, c, c0:c0 + P], l[:, c, c0:c0 + P], uT_h[:, c, :], uT_l[:, c, :], c == 0, c == KC - 1)
                return last

            def rows_proj(dst, t, wh, wl):
                for c in range(KC):
                    last = mm3(dst, uT_h[:, c, t * P:t * P + P], uT_l[:, c, t * P:t * P + P],
                               wh(c), wl(c), c == 0, c == KC - 1)
                return last

            for k in range(4):
                h, l = views(U_GLU + k, 8)
                if k == 3:
                    pe.wait_ge(vec_sb, 2)
                for i in range(2):
                    last = cols_proj(ps[:, 4 + k, i * S:i * S + S], h, l, i * P)
                last.then_inc(unit_used, 1)
            h, l = views(U_CMP_IN, 8)
            for kv in range(2):
                last = cols_proj(ps[:, 2, kv * S:kv * S + S], h, l, kv * P)
            last.then_inc(unit_used, 1)
            for u in range(2):
                h, l = views(U_Q + u, 8)
                for j in range(2):
                    last = cols_proj(ps[:, u, j * S:j * S + S], h, l, j * P)
                last.then_inc(unit_used, 1)

            def to_both(dst, k):
                for g in range(2):
                    last = t_.matmul(dst[:, g * S:g * S + S], both[:, g, :], ktmp[:, k, :], start=True, stop=True)
                return last

            pe.wait_ge(consts, 5)
            pe.wait_ge(proj_sb, 1)
            pe.wait_ge(glu_sb, 2)
            to_both(ps[:, 4, :], 0)
            to_both(ps[:, 6, :], 1).then_inc(dup_ps, 1)
            for u in range(2):
                h, l = views(U_SLC + u, 8)
                if u == 0:
                    pe.wait_ge(glu_sig, 2)
                cols_proj(ps[:, (3, 7)[u], 0:S], h, l, 0)
                for t in range(T):
                    last = rows_proj(ps[:, (5, 2)[u], t * P:t * P + P], t,
                                     lambda c: h[:, c, P:2 * P], lambda c: l[:, c, P:2 * P])
                last.then_inc(unit_used, 1)
            pe.wait_ge(wg_lo, 1)
            pe.wait_ge(proj_sb, 2)
            gh, gl = (ht[:, i, 0:KC * GATES].rearrange("p (c n) -> p c n", c=KC) for i in range(2))
            for t in range(T):
                last = rows_proj(ps[:, 0, t * GATES:t * GATES + GATES], t, lambda c: gh[:, c, :], lambda c: gl[:, c, :])
            last.then_inc(gates_ps, 1)
            pe.wait_ge(proj_sb, 7)
            pe.wait_ge(xcmp_sb, 1)
            to_both(ps[:, 4, :], 2)
            to_both(ps[:, 6, :], 3).then_inc(dup_ps, 1)

            pe.wait_ge(xcl_done, 1)
            for j in range(4):
                kv = j // 2
                h, l = views(U_CW1 + j, 8)
                for c in range(8):
                    cx = 8 * (j % 2) + c
                    last = mm3(ps[0:NG, HIDDEN[kv], 0:CMP_HID], xc_h[:, kv, cx, :], xc_l[:, kv, cx, :],
                               h[:, c, :], l[:, c, :], cx == 0, cx == 15)
                last.then_inc(unit_used, 1)
            for kv in range(2):
                pe.wait_ge(hn_sb, kv + 1)
                if kv == 1:
                    pe.wait_ge(proj_sb, 9)
                for hh in range(2):
                    last = t_.transpose(ps[:, (2, 6)[kv], hh * NG:hh * NG + NG], hnat[0:NG, kv, hh * P:hh * P + P],
                                        ident[0:NG, 0:NG])
                last.then_inc(hcT_ps, 1)
            pe.wait_ge(hc_sb, 2)
            for hh in range(2):
                last = t_.matmul(ps[:, 5, 0:NG], w2k[:, hh, :], hc[:, 0, hh, :], start=hh == 0, stop=hh == 1)
            last.then_inc(kv_ps, 1)
            pe.wait_ge(hc_sb, 4)
            for g in range(2):
                for hh in range(2):
                    last = t_.matmul(ps[0:NCMP, 4, g * HD:g * HD + HD], hc[:, 1, hh, g * NCMP:g * NCMP + NCMP],
                                     w2v[:, hh, :], start=hh == 0, stop=hh == 1)
            last.then_inc(kv_ps, 1)

            pe.wait_ge(kc_sb, 1)
            pe.wait_ge(proj_sb, 10)
            for i in range(2):
                for g in range(2):
                    for j in range(2):
                        for f in range(2):
                            q = i * 4 + 2 * g + j
                            fs = slice(HD * f, HD * f + HD)
                            last = t_.matmul(ps[:, f, q * NCMP:q * NCMP + NCMP], qT[fs, 2 * g + j, i * P:i * P + P],
                                             kcT[fs, g * NCMP:g * NCMP + NCMP], start=True, stop=True)
            last.then_inc(sc_ps, 1)
            pe.wait_ge(conv_vec, 1)
            pe.wait_ge(conv_pool, 1)
            for t in range(T):
                for cc in range(CC):
                    last = t_.transpose(ps[:, 2 + t, cc * P:cc * P + P], yT[:, cc, t * P:t * P + P], ident[:, :])
                last.then_inc(cn_ps, 1)
            pe.wait_ge(pc_sb, 1)
            pe.wait_ge(vc_sb, 1)
            for q in range(16):
                last = t_.transpose(ps[0:NCMP, 4 + q // 4, (q % 4) * P:(q % 4) * P + P],
                                    atmp[:, q * NCMP:q * NCMP + NCMP], ident[:, :])
                if q % 4 == 3:
                    last.then_inc(pcT_ps, 1)
            pe.wait_ge(pcT_sb, 4)
            for i in range(2):
                for q in range(4):
                    for f in range(2):
                        h = 2 * q + f
                        last = t_.matmul(ps[:, i, h * HD:h * HD + HD], pcT[0:NCMP, f * 8 + i * 4 + q, :],
                                         vc[0:NCMP, q // 2, :], start=True, stop=True)
                last.then_inc(oc_ps, 1)

            pe.wait_ge(cn_sb, 2)
            for cc in range(CC):
                for t in range(T):
                    last = t_.transpose(ps[:, 4 + cc // 2, (cc % 2) * S + t * P:(cc % 2) * S + t * P + P],
                                        cn[:, t, cc * P:cc * P + P], ident[:, :])
                if cc % 2:
                    last.then_inc(cnT_ps, 1)

            def scores(m):
                br, g, i = m // 4, m // 2 % 2, m % 2
                nk = P * (i + 1)
                if m < 2:
                    pe.wait_ge(sc_sb, 1)
                    pe.wait_ge(oc_sb, 2)
                else:
                    pe.wait_ge(s_sb, m - 1)
                for f in range(2):
                    for j in range(2):
                        fs = slice(HD * f, HD * f + HD)
                        last = t_.matmul(ps[:, 2 * i + f, j * nk:j * nk + nk], qT[fs, 2 * g + j, i * P:i * P + P],
                                         kT[br][fs, g, 0:nk], start=True, stop=True)
                last.then_inc(s_ps, 1)

            scores(0)
            for m in range(8):
                br, g, i = m // 4, m // 2 % 2, m % 2
                nk = P * (i + 1)
                pr = prob[:, i * 1024:i * 1024 + 4 * nk]
                if m < 7:
                    scores(m + 1)
                pe.wait_ge(p_sb, m + 1)
                if m == 0:
                    pe.wait_ge(mh_done, 2)
                for s in range(4 * (i + 1)):
                    last = t_.transpose(ps[:, 4 + s // 4, (s % 4) * P:(s % 4) * P + P], pr[:, s * P:s * P + P], ident[:, :])
                last.then_inc(pT_ps, 1)
                pe.wait_ge(pT_sbA, m + 1)
                if i:
                    pe.wait_ge(pT_sbV, m // 2 + 1)
                if m >= 2:
                    pe.wait_ge(o_sb, m - 1)
                for j in range(2):
                    for f in range(2):
                        hh = 2 * j + f
                        for kb in range(i + 1):
                            s = (2 * f + j) * (i + 1) + kb
                            last = t_.matmul(ps[:, 6 + i, hh * HD:hh * HD + HD], probT[:, s * P:s * P + P],
                                             vv[br][:, kb, g * HD:g * HD + HD], start=kb == 0, stop=kb == i)
                last.then_inc(o_ps, 1)

            pe.wait_ge(o_sb, 8)
            for c in range(4):
                for t in range(T):
                    last = t_.transpose(ps[:, 4 + c // 2, (c % 2) * S + t * P:(c % 2) * S + t * P + P],
                                        oacc[:, t, c * P:c * P + P], ident[:, :])
                if c % 2:
                    last.then_inc(oT_ps, 1)
            pe.wait_ge(ml_done, 4)
            out_proj(U_OUT0, None)

            pe.wait_ge(x_new, 2)
            pre_norm(1)
            pe.wait_ge(ul_done, 8)

            def ffn_gu(b, k, half, it=0):
                h, l = (w.rearrange("p (c n) -> p c n", c=4) for w in unit(k, it))
                for t in range(T):
                    for cc in range(4):
                        c = 4 * half + cc
                        last = mm3(ps[:, 4 + t, :], uT_h[:, c, t * P:t * P + P], uT_l[:, c, t * P:t * P + P],
                                   h[:, cc, :], l[:, cc, :], c == 0, c == KC - 1)
                last.then_inc(unit_used, 1)

            def ffn_T(b):
                pe.wait_ge(h_done, 2 * b + 2)
                for c in range(2):
                    for t in range(T):
                        last = t_.transpose(ps[:, 6, c * S + t * P:c * S + t * P + P],
                                            hbuf[:, t * 256 + c * P:t * 256 + c * P + P], ident[:, :])
                last.then_inc(hT_ps, 1)

            def ffn_down(b, k, it=0, first=False, final=False):
                h, l = views(k, 2, it)
                pe.wait_ge(hl_done, b + 1)
                for c in range(2):
                    for t in range(T):
                        for q in range(2):
                            last = mm3(ps[:, 2 * t + q, :], ht[:, 0, c * S + t * P:c * S + t * P + P],
                                       ht[:, 1, c * S + t * P:c * S + t * P + P],
                                       h[:, c, q * 512:q * 512 + 512], l[:, c, q * 512:q * 512 + 512],
                                       first and c == 0, final and c == 1)
                last.then_inc(unit_used, 1)

            k = U_FFN
            ffn_gu(0, k, 0)
            ffn_gu(0, k + 1, 1)
            ffn_T(0)
            ffn_gu(1, k + 2, 0)
            ffn_gu(1, k + 3, 1)
            ffn_down(0, k + 4, first=True)
            ffn_T(1)
            with pe.Fori(0, 3) as it:
                for j in range(3):
                    k = U_FFN + 5 + 3 * j
                    b = it * 3 + (FFN_LOOP0 + j)
                    ffn_gu(b, k, 0, it)
                    ffn_gu(b, k + 1, 1, it)
                    ffn_down(b - 1, k + 2, it)
                    ffn_T(b)
            ffn_down(FFN_BLOCKS - 1, U_GM - 1, final=True)

            pe.wait_ge(x_new, 4)
            pre_norm(2)
            pe.wait_ge(ul_done, 12)
            pe.wait_ge(ws_masked, 1)
            for g in range(8):
                last = t_.transpose(ps[:, g // 4, (g % 4) * P:(g % 4) * P + P], ws[:, g, :], ident[:, :])
                if g % 4 == 3:
                    last.then_inc(wsT_ps, 1)
            for cb in range(4):
                if cb >= 2:
                    pe.wait_ge(z_sb, 2 * (cb - 1))
                for a in range(2):
                    h, l = views(U_GM + 2 * cb + a, 4)
                    for t in range(T):
                        for cc in range(4):
                            c = 4 * a + cc
                            last = mm3(ps[:, 4 + 2 * (cb % 2) + t, :], uT_h[:, c, t * P:t * P + P],
                                       uT_l[:, c, t * P:t * P + P], h[:, cc, :], l[:, cc, :], c == 0, c == KC - 1)
                    last.then_inc(unit_used, 1)
            pe.wait_ge(wsT_sb, 2)
            for t in range(T):
                pe.wait_ge(z2_done, t + 1)
                for g in range(8):
                    last = t_.matmul(ps[:, 2 * t + g // 4, (g % 4) * P:(g % 4) * P + P], wsT[:, g, :],
                                     z2[:, t, g * P:g * P + P], start=True, stop=True)
                    if g % 4 == 3:
                        last.then_inc(mixed_ps, 1)
            pe.wait_ge(gy_done, 4)
            pe.wait_ge(z_sb, 8)
            for c in range(8):
                for t in range(T):
                    last = t_.transpose(ps[:, 4 + c // 2, (c % 2) * S + t * P:(c % 2) * S + t * P + P],
                                        z1[:, t, c * P:c * P + P], ident[:, :])
                if c % 2:
                    last.then_inc(gyT_ps, 1)
            pe.wait_ge(gl_done, 4)
            out_proj(U_GMO, None)

            pe.wait_ge(x_new, 6)
            pre_norm(3)
            pe.wait_ge(ul_done, 16)
            pe.wait_ge(wr_lo, 1)
            rh, rl = (ht[:, i, 0:KC * NE].rearrange("p (c n) -> p c n", c=KC) for i in range(2))
            for t in range(T):
                last = rows_proj(ps[:, 4, t * NE:t * NE + NE], t, lambda c: rh[:, c, :], lambda c: rl[:, c, :])
            last.then_inc(lg_ps, 1)
            pe.wait_ge(m_done, 1)
            pe.wait_ge(route_consts, 3)
            mk = rt[:, 80:96].rearrange("p (t e) -> p t e", t=T)
            t_.matmul(ps[:, 5, 0:NE], tri[:, :], mk[:, 0, :], start=True, stop=True)
            t_.matmul(ps[:, 5, NE:2 * NE], tri[:, :], mk[:, 1, :], start=True, stop=False)
            t_.matmul(ps[:, 5, NE:2 * NE], ones[:, :], mk[:, 0, :], start=False, stop=True)
            t_.matmul(ps[:, 5, 2 * NE:3 * NE], ones[:, :], mk[:, 0, :], start=True, stop=False)
            t_.matmul(ps[:, 5, 2 * NE:3 * NE], ones[:, :], mk[:, 1, :], start=False, stop=True).then_inc(pos_ps, 1)

            def gather(e, nt):
                w = nt * P
                pe.wait_ge(sel_done, e + 1)
                for c in range(KC):
                    bank, o = 4 + c * w // 512, c * w % 512
                    for t in range(T):
                        last = t_.matmul(ps[:, bank, o:o + w], xres[:, t, c * P:c * P + P],
                                         selr[:, t, 0:w], start=t == 0, stop=t == 1)
                last.then_inc(gath_ps, 1)

            def combine(e, nt):
                pe.wait_ge(pt_sb, e + 1)
                pe.wait_ge(yl_done, 2 * e + 2)
                for t in range(T):
                    for q in range(2):
                        for i in range(nt):
                            for part in range(2):
                                last = t_.matmul(ps[:, (2, 0)[t] + q, :], pt01[:, i, t * P:t * P + P],
                                                 y_part(part, i, q), start=i + part == 0,
                                                 stop=i == nt - 1 and part == 1)
                        last.then_inc(comb_ps[2 * t + q], 1)

            def blocks(e, j, it, nt):
                pe.wait_ge(xgl_done, e + 1)
                for i in range(nt):
                    for t in range(T):
                        last = t_.transpose(ps[:, 4, i * S + t * P:i * S + t * P + P],
                                            sel01[:, t, i * P:i * P + P], ident[:, :])
                last.then_inc(pt_ps, 1)
                w = nt * P

                def moe_unit(m, c):
                    m += MOE_UNITS * j
                    pe.wait_ge(lo_done, U_MOE + m + 1 + 2 * MOE_UNITS * it)
                    s = (U_MOE + m) % PARTS
                    return (w_[:, s, :].rearrange("p (c n) -> p c n", c=c) for w_ in (w_hi, w_lo))

                def down(b, m):
                    pe.wait_ge(mhl_done, MOE_BLOCKS * e + (b + 1))
                    if b == 0:
                        pe.wait_ge(acc_done, 4 * e)
                    for a in range(2):
                        h, l = moe_unit(m + a, 2)
                        for cc in range(2):
                            c = 2 * a + cc
                            for i in range(nt):
                                o = 512 * i + c * P
                                for q in range(2):
                                    last = mm3(ps[:, 2 * i + q, :], ht[:, 0, o:o + P], ht[:, 1, o:o + P],
                                               h[:, cc, q * 512:q * 512 + 512], l[:, cc, q * 512:q * 512 + 512],
                                               b == 0 and c == 0, b == MOE_BLOCKS - 1 and c == 3)
                        last.then_inc(unit_used, 1)

                m = 0
                for b in range(MOE_BLOCKS):
                    for u in (1, 0):
                        if u == 0:
                            if b == 0:
                                pe.wait_ge(pt_sb, e + 1)
                            else:
                                pe.wait_ge(mhl_done, MOE_BLOCKS * e + b)
                        for a in range(2):
                            h, l = moe_unit(m, 4)
                            for i in range(nt):
                                for cc in range(4):
                                    c = 4 * a + cc
                                    o = c * w + i * P
                                    last = mm3(ps[:, 4 + 2 * i + u, :], ra[:, o:o + P], ra[:, 2048 + o:2048 + o + P],
                                               h[:, cc, :], l[:, cc, :], c == 0, c == KC - 1)
                            last.then_inc(unit_used, 1)
                            m += 1
                    if b:
                        down(b - 1, m)
                        m += 2
                    pe.wait_ge(mh_ok, MOE_BLOCKS * e + (b + 1))
                    for i in range(nt):
                        for c in range(4):
                            last = t_.transpose(ps[:, 4 + 2 * i, c * P:c * P + P], eh[:, i, c * P:c * P + P], ident[:, :])
                    last.then_inc(mhT_ps, 1)
                down(MOE_BLOCKS - 1, m)

            pe.wait_ge(routed, 1)
            with pe.Fori(0, NE // 2) as it:
                for j in range(2):
                    e = 2 * it + j
                    two = pe.value_load(flag[0:1, bass.ds(e, 1)], min_val=0, max_val=1)
                    last_e = pe.value_load(flag[0:1, bass.ds(e + NE, 1)], min_val=0, max_val=2)
                    for nt in (1, 2):
                        with pe.If(two == nt - 1):
                            gather(e, nt)
                    for nt in (1, 2):
                        with pe.If(last_e == nt):
                            combine(e - 1, nt)
                    for nt in (1, 2):
                        with pe.If(two == nt - 1):
                            blocks(e, j, it, nt)
            last_e = pe.value_load(flag[0:1, 2 * NE:2 * NE + 1], min_val=0, max_val=2)
            for nt in (1, 2):
                with pe.If(last_e == nt):
                    combine(NE - 1, nt)


_INS = ['x', 'norm_mix_pre', 'norm_mix_post', 'norm_ffn_pre', 'norm_ffn_post', 'nsa_conv_w_in', 'cmp_pe',
        'cmp_w1', 'cmp_b1', 'cmp_w2', 'cmp_b2', 'conv_w', 'conv_b', 'conv_ln_g', 'conv_ln_b',
        'nsa_conv_w_out', 'ffn_w_gate', 'ffn_w_up', 'ffn_w_down', 'gmlp_w_in', 'gmlp_ln_g', 'gmlp_ln_b',
        'gmlp_w_s', 'gmlp_b_s', 'gmlp_w_out', 'moe_w_router', 'moe_w_gate', 'moe_w_up', 'moe_w_down']


def kernel(**inputs):
    import numpy as np
    import concourse.bacc as bacc
    from concourse.bass_utils import run_bass_kernel_spmd

    nc = bacc.Bacc("TRN2", target_bir_lowering=False, num_devices=1)
    arrays, args = {}, []
    for name in _INS:
        a = np.ascontiguousarray(inputs[name])
        arrays[f"in_{name}"] = a
        args.append(nc.dram_tensor(f"in_{name}", a.shape, mybir.dt.from_np(a.dtype), kind="ExternalInput").ap())
    args.append(nc.dram_tensor("out", (1, S, D), F32, kind="ExternalOutput").ap())
    program(nc, *args)
    r = run_bass_kernel_spmd(nc, [arrays], core_ids=[0])
    return r.results[0]["out"]
```

```python
from contextlib import ExitStack

import concourse.bass as bass
from concourse import mybir

F32 = mybir.dt.float32
F32R = mybir.dt.float32r
I32 = mybir.dt.int32
ALU = mybir.AluOpType
ACT = mybir.ActivationFunctionType
AX = mybir.AxisListType

P = 128
T = 2
S = T * P
D = 1024
KC = D // P
HEADS, KV_HEADS, HD = 8, 2, 64
HPG = HEADS // KV_HEADS
QC = HEADS * HD
KVC = 3 * 2 * KV_HEADS * HD
GATES = 3 * HEADS
CONV_CH, CONV_W = 512, 31
CC = CONV_CH // P
CMP_LEN, CMP_STRIDE, CMP_HID = 32, 16, 256
NCMP = (S - CMP_LEN) // CMP_STRIDE + 1
NG = KV_HEADS * NCMP
FF = 2816
FFN_BLOCKS = FF // 256
GM = 1024
NE = 8
EFF = 3584
MOE_BLOCKS = EFF // 512
HALF = P // 2
KINDS = ((False,), (False, True), (False, False))
KIND_LIMITS = (P, P + HALF)
EPS = 1e-6
NEG = -1e30

UF = 2048
SLOTS = 14
RING1 = 9
RING2 = 12
SCRATCH = SLOTS - RING1
PARTS = 3
U_GLU, U_CMP_IN, U_Q, U_SLC, U_WIN, U_CW1, U_OUT0 = 0, 4, 5, 7, 8, 9, 13
U_FFN = 17
U_GM = U_FFN + 3 * FFN_BLOCKS
U_GMO = U_GM + 8
U_MOE = U_GMO + 4
MOE_UNITS = 6 * MOE_BLOCKS
HIDDEN = (1, 3)
FFN_LOOP0 = 2
assert 2 * MOE_UNITS % RING2 == 0 and MOE_UNITS % PARTS == 0 and 9 % RING1 == 0 and 9 % PARTS == 0

V_MIX, V_FFN, V_CB, V_CG, V_CLB, V_B1, V_PE, V_BS, V_B2K = 0, 16, 32, 36, 40, 44, 48, 80, 88
V_ROWS = 89
VEC_LOADS = 11
SMALL_LOADS = 5


def moe_slot(m):
    m %= RING2
    new = RING2 - RING1
    return RING1 + m if m < new else (U_MOE + m - new) % RING1


def unit_dmas(k):
    if U_FFN <= k < U_GM:
        j = k - U_FFN
        return 1 if j == 32 or (j >= 4 and (j - 2) % 3 == 2) else 2
    return 1


def raw_slot(k):
    return k % RING1 if k < U_MOE else moe_slot(k - U_MOE)


def raw_count(k):
    return 16 * sum(unit_dmas(i) for i in range(k % RING1, k + 1, RING1))


def moe_count(m):
    s = moe_slot(m)
    before = 0 if s >= RING1 else raw_count(max(k for k in range(U_MOE) if k % RING1 == s))
    return before + 16 * (m // RING2 + 1)


def program(nc, x, norm_mix_pre, norm_mix_post, norm_ffn_pre, norm_ffn_post, nsa_conv_w_in, cmp_pe,
            cmp_w1, cmp_b1, cmp_w2, cmp_b2, conv_w, conv_b, conv_ln_g, conv_ln_b, nsa_conv_w_out,
            ffn_w_gate, ffn_w_up, ffn_w_down, gmlp_w_in, gmlp_ln_g, gmlp_ln_b, gmlp_w_s, gmlp_b_s,
            gmlp_w_out, moe_w_router, moe_w_gate, moe_w_up, moe_w_down, out):
    ctx = ExitStack()
    with ctx:
        def sb(name, shape, dt=F32):
            return ctx.enter_context(nc.sbuf_tensor(name, shape, dt))

        def sem(name):
            return ctx.enter_context(nc.semaphore(name))

        raw = sb("raw", [P, SLOTS, UF])
        w_hi = sb("w_hi", [P, PARTS, UF], F32R)
        w_lo = sb("w_lo", [P, PARTS, UF], F32R)
        xres = sb("xres", [P, T, D])
        xn = sb("xn", [P, T, D])
        gpost = sb("gpost", [P, D])
        ra = sb("ra", [P, 4 * 1024], F32R)
        ht = sb("ht", [P, 2, 1024], F32R)
        pt01 = sb("pt01", [P, 2, S], F32R)
        ident = sb("ident", [P, P])
        vec = sb("vec", [P, V_ROWS])
        st = sb("st", [P, 80])
        neg_half = sb("neg_half", [P, 2])
        router = sb("router", [P, KC * NE])
        warm = sb("warm", [P, 1])
        flag = sb("flag", [P, 2 * NE + 1], I32)
        ps = ctx.enter_context(nc.psum_tensor("ps", [P, 8, 512], F32))

        uT_h = ra[:, 0:2048].rearrange("p (c t) -> p c t", c=KC)
        uT_l = ra[:, 2048:4096].rearrange("p (c t) -> p c t", c=KC)

        area = raw[:, RING1:SLOTS, :].rearrange("p s f -> p (s f)")
        at = [0]

        def take(n):
            at[0] += n
            assert at[0] <= SCRATCH * UF
            return area[:, at[0] - n:at[0]]

        prob = take(2048)
        probT = take(1024)
        qT = take(1024).rearrange("p (c t) -> p c t", c=4)
        kT = [take(512).rearrange("p (g t) -> p g t", g=2) for _ in range(2)]
        vv = [take(256).rearrange("p (t n) -> p t n", t=T) for _ in range(2)]
        PADT = CONV_W - 1 + S
        cT = take(CC * PADT).rearrange("p (c t) -> p c t", c=CC)
        yT = take(CC * S).rearrange("p (c t) -> p c t", c=CC)
        mask = take(S)
        vec_rows = take(P)
        cw_rows = take(P)
        cw = take(CC * CONV_W)
        w2k = take(256).rearrange("p (h n) -> p h n", h=2)
        w2v = take(128).rearrange("p (h n) -> p h n", h=2)
        wgate = take(KC * GATES)
        gates = take(T * GATES).rearrange("p (t n) -> p t n", t=T)
        hc = take(4 * NG).rearrange("p (k h n) -> p k h n", k=2, h=2)
        kcT = take(NG)
        vc = take(2 * HD).rearrange("p (g d) -> p g d", g=2)
        b2v = take(HD)
        cadd = take(2 * NCMP).rearrange("p (i n) -> p i n", i=2)
        cmul = take(2 * NCMP).rearrange("p (i n) -> p i n", i=2)
        ptmp = take(S)
        atmp = take(S)
        both = take(2 * P).rearrange("p (g n) -> p g n", g=2)
        ktmp = prob[:, 0:4 * S].rearrange("p (k t) -> p k t", k=4)
        xcmp = probT[:, 0:4 * 240].rearrange("p (k c g n) -> p k c g n", k=2, c=16, g=2)
        xc_h = ra[:, 0:960].rearrange("p (k c n) -> p k c n", k=2, c=16)
        xc_l = ra[:, 1024:1984].rearrange("p (k c n) -> p k c n", k=2, c=16)
        y2 = cT[:, :, 0:S]
        hnat = prob[:, 1024:1536].rearrange("p (k n) -> p k n", k=2)
        pcT = prob[:, 0:2048].rearrange("p (q t) -> p q t", q=16)
        oacc = xn[:, 0, :].rearrange("p (i n) -> p i n", i=T)
        cn = xn[:, 1, :].rearrange("p (i n) -> p i n", i=T)

        z1 = area[:, 0:2048].rearrange("p (t n) -> p t n", t=T)
        z2 = area[:, 2048:4096].rearrange("p (t n) -> p t n", t=T)
        ws = area[:, 4096:5120].rearrange("p (g s) -> p g s", g=8)
        wsT = area[:, 5120:6144].rearrange("p (g s) -> p g s", g=8)
        ln_g = area[:, 6144:7168]
        ln_b = area[:, 7168:8192]

        sg, hbuf = area[:, 8192:8704], area[:, 8704:9216]
        iota, tri, ones = area[:, 6144:6400], area[:, 6400:6528], area[:, 6528:6656]
        sel01 = area[:, 7168:7680].rearrange("p (t j) -> p t j", t=T)
        selr = area[:, 7680:8192].rearrange("p (t j) -> p t j", t=T)
        gfin = area[:, 7168:8192]
        esg = area[:, 8192:9216].rearrange("p (i n) -> p i n", i=2)
        eh = area[:, 9216:10240].rearrange("p (i n) -> p i n", i=2)
        lgT = eh[:, 0, 0:S]
        rt = gpost[:, 576:1024]
        acc = xn

        def x_part(part, i, c, packed):
            o = 1024 * i + P * c
            if packed:
                return ra[:, o + HALF * part:o + HALF * part + HALF]
            return ra[:, o + 2048 * part:o + 2048 * part + P]

        def x_tile(part, i, c):
            o = 1024 * i + 2048 * part + P * c
            return ra[:, o:o + P]

        def gate_bank(b, i, nt):
            return 4 + 2 * (b % 2 if nt == 1 else i)

        def halves(a):
            return a.rearrange("p (c h n) -> p c h n", c=4, h=2)

        def y_part(part, i, q):
            if i:
                return ht[:, part, 512 * q:512 * q + 512]
            return ra[:, 2048 * part + 1024 + 512 * q:2048 * part + 1536 + 512 * q]

        raw_in = [sem(f"raw_in{i}") for i in range(SLOTS)]
        hi_done, lo_done, unit_used = sem("hi_done"), sem("lo_done"), sem("unit_used")
        x_in, vec_in, small_in, post_in, gm_in = sem("x_in"), sem("vec_in"), sem("small_in"), sem("post_in"), sem("gm_in")
        router_in, stored = sem("router_in"), sem("stored")
        consts, vec_ps, vec_sb = sem("consts"), sem("vec_ps"), sem("vec_sb")
        ss_done, xn_done, xT_ps = sem("ss_done"), sem("xn_done"), sem("xT_ps")
        uh_done, ul_done, x_new = sem("uh_done"), sem("ul_done"), sem("x_new")
        ws_in, route_consts = sem("ws_in"), sem("route_consts")
        dup_ps, rs_in, rs_out = sem("dup_ps"), sem("rs_in"), sem("rs_out")
        wg_hi, wg_lo, gates_ps, gT_sb = sem("wg_hi"), sem("wg_lo"), sem("gates_ps"), sem("gT_sb")
        proj_sb, xcmp_sb, glu_sig, glu_sb = sem("proj_sb"), sem("xcmp_sb"), sem("glu_sig"), sem("glu_sb")
        xch_done, xcl_done, hc_sb = sem("xch_done"), sem("xcl_done"), sem("hc_sb")
        hn_sb, hcT_ps = sem("hn_sb"), sem("hcT_ps")
        kv_ps, kc_sb, vc_sb = sem("kv_ps"), sem("kc_sb"), sem("vc_sb")
        sc_ps, sc_sb, ex_sb, pc_sb = sem("sc_ps"), sem("sc_sb"), sem("ex_sb"), sem("pc_sb")
        pcT_ps, pcT_sb, oc_ps, oc_sb = sem("pcT_ps"), sem("pcT_sb"), sem("oc_ps"), sem("oc_sb")
        s_ps, s_sb, p_sb, pT_ps = sem("s_ps"), sem("s_sb"), sem("p_sb"), sem("pT_ps")
        pT_sb, o_ps, o_sb = sem("pT_sb"), sem("o_ps"), sem("o_sb")
        conv_pool, conv_vec = sem("conv_pool"), sem("conv_vec")
        cn_ps, cn_sb, cnT_ps, y2_sb = sem("cn_ps"), sem("cn_sb"), sem("cnT_ps"), sem("y2_sb")
        oT_ps, mh_done, ml_done = sem("oT_ps"), sem("mh_done"), sem("ml_done")
        pss_done, tile0_ps = sem("pss_done"), sem("tile0_ps")
        sg_done, h_done, hT_ps, hh_done, hl_done = (
            sem("sg_done"), sem("h_done"), sem("hT_ps"), sem("hh_done"), sem("hl_done"))
        ws_masked, wsT_ps, wsT_sb, z_sb = sem("ws_masked"), sem("wsT_ps"), sem("wsT_sb"), sem("z_sb")
        z2_done, mixed_ps, gy_done, gyT_ps = sem("z2_done"), sem("mixed_ps"), sem("gy_done"), sem("gyT_ps")
        gh_done, gl_done = sem("gh_done"), sem("gl_done")
        lgT_sb = sem("lgT_sb")
        wr_hi, wr_lo, lg_ps, ex_in, ex_out = sem("wr_hi"), sem("wr_lo"), sem("lg_ps"), sem("ex_in"), sem("ex_out")
        m_done, pos_ps, routed = sem("m_done"), sem("pos_ps"), sem("routed")
        sel_done, gath_ps, xgh_done, xgl_done = sem("sel_done"), sem("gath_ps"), sem("xgh_done"), sem("xgl_done")
        pt_ps, pt_sb = sem("pt_ps"), sem("pt_sb")
        msg_done, mh_ok, mhT_ps, mhh_done, mhl_done = (
            sem("msg_done"), sem("mh_ok"), sem("mhT_ps"), sem("mhh_done"), sem("mhl_done"))
        yh_done = [sem(f"yh_done{q}") for q in range(2)]
        comb_ps = [sem(f"comb_ps{k}") for k in range(2 * T)]
        yl_done, acc_done = sem("yl_done"), sem("acc_done")
        act_chain, dve_chain, pool_chain = sem("act_chain"), sem("dve_chain"), sem("pool_chain")

        class Chain:

            def __init__(self, eng, s):
                self.eng, self.sem, self.n, self.more = eng, s, 0, 0

            def link(self, ins):
                ins.then_inc(self.sem, 1)
                self.n += 1
                self.wait()

            def add(self, ins):
                ins.then_inc(self.sem, 1)
                self.n += 1

            def wait(self):
                self.eng.wait_ge(self.sem, self.n + self.more)

        def wait_raw(eng, k, it=0):
            eng.wait_ge(raw_in[raw_slot(k)], raw_count(k) + 16 * unit_dmas(k) * it)

        block = ctx.enter_context(nc.Block())

        @block.sync
        def _(sp):
            sp.dma_start(xres[:, :, :], x[0].rearrange("(t p) d -> p t d", p=P)).then_inc(x_in, 16)
            rows = [(V_MIX, norm_mix_pre.rearrange("l (c p) -> (l c) p", p=P)),
                    (V_FFN, norm_ffn_pre.rearrange("l (c p) -> (l c) p", p=P)),
                    (V_CB, conv_b.rearrange("o (c p) -> (o c) p", p=P)),
                    (V_CG, conv_ln_g.rearrange("o (c p) -> (o c) p", p=P)),
                    (V_CLB, conv_ln_b.rearrange("o (c p) -> (o c) p", p=P)),
                    (V_B1, cmp_b1.rearrange("o k (c p) -> (o k c) p", p=P)),
                    (V_PE, cmp_pe.rearrange("o k (c r) d -> (o k c) (r d)", r=2)),
                    (V_BS, gmlp_b_s.rearrange("o g t -> (o g) t"))]
            assert len(rows) + 3 == VEC_LOADS
            for r, src in rows:
                sp.dma_start(vec_rows[r:r + src.shape[0], :], src).then_inc(vec_in, 16)
            for h in range(2):
                sp.dma_start(vec_rows[V_B2K:V_B2K + 1, h * HD:h * HD + HD], cmp_b2[:, 0, :]).then_inc(vec_in, 16)
            sp.dma_start(cw_rows[0:CC * CONV_W, :],
                         conv_w.rearrange("o w i (c p) -> (o w i c) p", p=P)).then_inc(vec_in, 16)

            def load(k, parts, it=0):
                if k >= RING1:
                    sp.wait_ge(lo_done, k - RING1 + 1 + 9 * it)
                for dst, src in parts:
                    sp.dma_start(dst, src).then_inc(raw_in[raw_slot(k)], 16)

            def slot(k, a):
                return raw[:, raw_slot(k), :].rearrange("p (c n) -> p c n", c=a)

            win = nsa_conv_w_in[0].rearrange("(c p) n -> p c n", p=P)
            g0 = QC + KVC + GATES
            cols = [g0, g0 + CONV_CH, g0 + 256, g0 + CONV_CH + 256, QC, 0, 256, QC + 256, QC + 512]
            for k, c0 in enumerate(cols):
                load(k, [(slot(k, 8), win[:, :, c0:c0 + 256])])
            for j in range(4):
                w1 = cmp_w1[0, j // 2].rearrange("(c p) n -> p c n", p=P)
                load(U_CW1 + j, [(slot(U_CW1 + j, 8), w1[:, 8 * (j % 2):8 * (j % 2) + 8, :])])
            wo = nsa_conv_w_out[0].rearrange("(c p) n -> p c n", p=P)
            for j in range(4):
                load(U_OUT0 + j, [(slot(U_OUT0 + j, 2), wo[:, 2 * j:2 * j + 2, :])])

            fg = ffn_w_gate[0].rearrange("(c p) n -> p c n", p=P)
            fu = ffn_w_up[0].rearrange("(c p) n -> p c n", p=P)
            fd = ffn_w_down[0].rearrange("(c p) n -> p c n", p=P)

            def load_gu(k, half, b, it=0):
                dst = raw[:, raw_slot(k), :].rearrange("p (c u n) -> p c u n", c=4, u=2)
                n0 = b * 256
                load(k, [(dst[:, :, u, :], w[:, 4 * half:4 * half + 4, bass.ds(n0, 256)])
                         for u, w in enumerate((fg, fu))], it)

            def load_down(k, b, it=0):
                load(k, [(slot(k, 2), fd[:, bass.ds(b * 2, 2), :])], it)

            k = U_FFN
            load_gu(k, 0, 0)
            load_gu(k + 1, 1, 0)
            load_gu(k + 2, 0, 1)
            load_gu(k + 3, 1, 1)
            load_down(k + 4, 0)
            with sp.Fori(0, 3) as it:
                for j in range(3):
                    k = U_FFN + 5 + 3 * j
                    b = it * 3 + (FFN_LOOP0 + j)
                    load_gu(k, 0, b, it)
                    load_gu(k + 1, 1, b, it)
                    load_down(k + 2, b - 1, it)
            load_down(U_GM - 1, FFN_BLOCKS - 1)

            gw = gmlp_w_in[0].rearrange("(c p) n -> p c n", p=P)
            for j in range(8):
                cb = (j // 2 + 2) % 4
                load(U_GM + j, [(slot(U_GM + j, 4), gw[:, 4 * (j % 2):4 * (j % 2) + 4, cb * 512:cb * 512 + 512])])
            go = gmlp_w_out[0].rearrange("(c p) n -> p c n", p=P)
            for j in range(4):
                load(U_GMO + j, [(slot(U_GMO + j, 2), go[:, 2 * j:2 * j + 2, :])])

            eg = moe_w_gate[0].rearrange("e (c p) n -> e p c n", p=P)
            eu = moe_w_up[0].rearrange("e (c p) n -> e p c n", p=P)
            ed = moe_w_down[0].rearrange("e (c p) n -> e p c n", p=P)

            def load_pair(it):
                m = 0

                def one(e, w, c0, n, col0, cols):
                    nonlocal m
                    sp.wait_ge(lo_done, U_MOE + m - RING2 + 1 + 2 * MOE_UNITS * it)
                    src = w[bass.ds(e, 1), :, c0:c0 + n, col0:col0 + cols].rearrange("o p c n -> (o p) c n")
                    sp.dma_start(slot(U_MOE + m, n), src).then_inc(raw_in[moe_slot(m)], 16)
                    m += 1

                for j in range(2):
                    e = 2 * it + j
                    for b in range(MOE_BLOCKS):
                        for w in (eu, eg):
                            for half in range(2):
                                one(e, w, 4 * half, 4, b * 512, 512)
                        if b:
                            for half in range(2):
                                one(e, ed, 4 * (b - 1) + 2 * half, 2, 0, D)
                    for half in range(2):
                        one(e, ed, 4 * (MOE_BLOCKS - 1) + 2 * half, 2, 0, D)

            sp.wait_ge(gyT_ps, 4)
            with sp.Fori(0, NE // 2) as it:
                load_pair(it)
            yo = out[0].rearrange("(t p) d -> p t d", p=P)
            for t in range(T):
                sp.wait_ge(x_new, 6 + t + 1)
                sp.dma_start(yo[:, t, :], xres[:, t, :]).then_inc(stored, 16)
            sp.wait_ge(stored, 16 * T)

        @block.gpsimd
        def _(pool):
            g = nc.gpsimd
            g.memset(ident[:, :], 0.0).then_inc(pool_chain, 1)
            g.memset(mask[:, :], 0.0).then_inc(pool_chain, 1)
            g.memset(cadd[:, :, :], 0.0).then_inc(pool_chain, 1)
            g.memset(cmul[:, :, :], 1.0).then_inc(pool_chain, 1)
            g.memset(cT[:, :, 0:CONV_W - 1], 0.0).then_inc(pool_chain, 1)
            g.memset(neg_half[:, :], -0.5).then_inc(pool_chain, 1)
            pool.wait_ge(pool_chain, 6)
            g.affine_select(out=ident[:, :], in_=ident[:, :], compare_op=ALU.not_equal, fill=1.0,
                            base=0, pattern=[[-1, P]], channel_multiplier=1).then_inc(consts, 1)
            g.affine_select(out=mask[:, P:S], in_=mask[:, P:S], compare_op=ALU.is_ge, fill=NEG,
                            base=0, pattern=[[-1, P]], channel_multiplier=1).then_inc(consts, 1)
            for m, fill in ((cadd, NEG), (cmul, 0.0)):
                g.affine_select(out=m[:, :, :], in_=m[:, :, :], compare_op=ALU.is_ge, fill=fill,
                                base=-(CMP_LEN - 1), pattern=[[P, 2], [-CMP_STRIDE, NCMP]],
                                channel_multiplier=1).then_inc(consts, 1)

            pool.wait_ge(consts, 4)
            for g_ in range(2):
                for h in range(2):
                    last = g.tensor_copy(both[:, g_, h * HD:h * HD + HD], ident[:, g_ * HD:g_ * HD + HD])
            last.then_inc(consts, 1)

            rs_n = [0]

            def power(c, w):
                rs_n[0] += 1
                pool.wait_ge(rs_in, rs_n[0])
                g.tensor_tensor(st[:, c:c + w], st[:, c:c + w], neg_half[:, 0:w], ALU.pow).then_inc(rs_out, 1)

            def powers(c):
                for t in range(T):
                    power(c + t, 1)

            powers(2)

            n = 6
            pool.wait_ge(glu_sb, 2)
            pool.wait_ge(vec_sb, 2)
            for cc in (3,):
                w = cw[:, cc:cc + 1]
                g.tensor_scalar(yT[:, cc, :], cT[:, cc, 0:S], w, vec[:, V_CB + cc:V_CB + cc + 1],
                                ALU.mult, ALU.add).then_inc(pool_chain, 1)
                n += 1
                for j in range(1, CONV_W):
                    w = cw[:, j * CC + cc:j * CC + cc + 1]
                    g.tensor_scalar(ptmp, cT[:, cc, j:j + S], w, None, ALU.mult).then_inc(pool_chain, 1)
                    n += 1
                    pool.wait_ge(pool_chain, n)
                    g.tensor_tensor(yT[:, cc, :], yT[:, cc, :], ptmp, ALU.add).then_inc(pool_chain, 1)
                    n += 1
                    pool.wait_ge(pool_chain, n)
            g.tensor_copy(ptmp[:, 0:1], yT[:, 3, 0:1]).then_inc(conv_pool, 1)

            for t in range(T):
                power(71 + 8 * t, 1)
            powers(6)
            powers(2)
            powers(6)
            powers(2)

            pool.wait_ge(ws_in, 16)
            g.affine_select(out=ws[:, :, :], in_=ws[:, :, :], compare_op=ALU.is_ge, fill=0.0,
                            base=0, pattern=[[0, 8], [-1, P]], channel_multiplier=1).then_inc(ws_masked, 1)
            for t in range(T):
                power(57, 1)
            pool.wait_ge(gyT_ps, 4)
            g.iota(iota, pattern=[[1, S]], base=0, channel_multiplier=0,
                   allow_small_or_imprecise_dtypes=True).then_inc(route_consts, 1)
            g.memset(ones, 1.0).then_inc(route_consts, 1)
            g.memset(eh[:, :, :], 0.0).then_inc(route_consts, 1)
            g.memset(tri, 1.0).then_inc(pool_chain, 1)
            pool.wait_ge(pool_chain, n + 1)
            g.affine_select(out=tri, in_=tri, compare_op=ALU.is_gt, fill=0.0,
                            base=0, pattern=[[1, P]], channel_multiplier=-1).then_inc(route_consts, 1)
            powers(6)
            powers(2)
            powers(6)

        @block.scalar
        def _(act):
            a = nc.scalar
            ch = Chain(act, act_chain)

            def split_hi(k, it=0):
                wait_raw(act, k, it)
                if k >= PARTS:
                    act.wait_ge(unit_used, k - PARTS + 1 + 9 * it)
                a.activation(w_hi[:, k % PARTS, :], raw[:, raw_slot(k), :], ACT.Copy).then_inc(hi_done, 1)

            def moe_hi(m, it):
                act.wait_ge(raw_in[moe_slot(m)], moe_count(m) + 16 * (2 * MOE_UNITS // RING2) * it)
                act.wait_ge(unit_used, U_MOE + m - PARTS + 1 + 2 * MOE_UNITS * it)
                a.activation(w_hi[:, (U_MOE + m) % PARTS, :], raw[:, moe_slot(m), :], ACT.Copy).then_inc(hi_done, 1)

            w2 = cmp_w2[0].rearrange("k (h p) n -> k p h n", p=P)
            for h in range(2):
                act.dma_start(w2k[:, :, h * HD:h * HD + HD], w2[0]).then_inc(small_in, 16)
            act.dma_start(w2v[:, :, :], w2[1]).then_inc(small_in, 16)
            act.dma_start(wgate.rearrange("p (c n) -> p c n", c=KC),
                          nsa_conv_w_in[0].rearrange("(c p) n -> p c n", p=P)[:, :, QC + KVC:QC + KVC + GATES]
                          ).then_inc(small_in, 16)
            act.dma_start(b2v[0:NCMP, :], cmp_b2[0, 1:2, :].partition_broadcast(NCMP)).then_inc(small_in, 16)
            act.dma_start(gpost[:, :], norm_mix_post[0:1, :].partition_broadcast(P)).then_inc(post_in, 16)

            def pre_norm(n, k=None, loads=()):
                for t in range(T):
                    if n == 0:
                        act.wait_ge(x_in, 16)
                    else:
                        act.wait_ge(x_new, 2 * (n - 1) + t + 1)
                    a.activation(xn[:, t, :], xres[:, t, :], ACT.Square,
                                 accum_out=st[:, t:t + 1]).then_inc(ss_done, 1)
                g0 = (V_MIX, V_FFN)[n % 2] + KC * (n // 2)
                if n == 0:
                    act.wait_ge(vec_sb, 1)
                for dst, src, s_ in loads:
                    act.dma_start(dst, src).then_inc(s_, 16)
                if k is not None:
                    split_hi(k)
                for c in range(KC):
                    if c % 2 == 0:
                        act.wait_ge(xT_ps, 4 * n + c // 2 + 1)
                    ins = a.activation(uT_h[:, c, :], ps[:, c // 2, (c % 2) * S:(c % 2) * S + S], ACT.Copy,
                                       scale=vec[:, g0 + c:g0 + c + 1])
                    if c % 2:
                        ins.then_inc(uh_done, 1)

            def post_norm(n, used=None):
                for t in range(T):
                    if n < 3:
                        if t == 0:
                            act.wait_ge(tile0_ps, n + 1)
                        else:
                            act.wait_ge(unit_used, used)
                        a.activation(xn[:, t, :].rearrange("p (h n) -> p h n", h=2), ps[:, 2 * t:2 * t + 2, :],
                                     ACT.Square, accum_out=st[:, 4 + t:5 + t]).then_inc(pss_done, 1)
                    else:
                        act.wait_ge(acc_done, 4 * (NE - 1) + 2 * (t + 1))
                        a.activation(ra[:, t * D:(t + 1) * D], acc[:, t, :],
                                     ACT.Square, accum_out=st[:, 4 + t:5 + t]).then_inc(pss_done, 1)

            pre_norm(0, 0)
            for k in range(1, 4):
                split_hi(k)
            act.wait_ge(small_in, 16 * SMALL_LOADS)
            a.activation(ht[:, 0, 0:KC * GATES], wgate, ACT.Copy).then_inc(wg_hi, 1)
            act.wait_ge(unit_used, 2)
            a.activation(yT[:, 0:2, :], ps[:, 5, :].rearrange("p (c t) -> p c t", c=2), ACT.Sigmoid).then_inc(glu_sig, 1)
            split_hi(4)
            split_hi(5)
            act.wait_ge(unit_used, 4)
            a.activation(yT[:, 2:4, :], ps[:, 7, :].rearrange("p (c t) -> p c t", c=2), ACT.Sigmoid).then_inc(glu_sig, 1)
            split_hi(6)
            act.wait_ge(unit_used, U_CMP_IN + 1)
            a.activation(ktmp[:, 0:2, :], ps[:, 2, :].rearrange("p (k t) -> p k t", k=2),
                         ACT.Copy).then_inc(proj_sb, 1)
            split_hi(7)
            for u in range(2):
                act.wait_ge(unit_used, U_Q + u + 1)
                a.activation(qT[:, 2 * u:2 * u + 2, :],
                             ps[:, u, :].rearrange("p (c t) -> p c t", c=2),
                             ACT.Copy, scale=float(HD) ** -0.5).then_inc(proj_sb, 1)
                split_hi(8 + u)
            for u in range(2):
                act.wait_ge(unit_used, U_SLC + u + 1)
                a.activation(ktmp[:, 2 + u, :], ps[:, (3, 7)[u], 0:S], ACT.Copy).then_inc(proj_sb, 1)
                a.activation(vv[u][:, :, :], ps[:, (5, 2)[u], 0:256].rearrange("p (t n) -> p t n", t=T),
                             ACT.Copy).then_inc(proj_sb, 1)
                split_hi(10 + u)
            act.wait_ge(xcmp_sb, 1)
            act.wait_ge(gates_ps, 1)
            a.activation(atmp[0:GATES, :], ps[0:GATES, 0, 0:S], ACT.Sigmoid).then_inc(gT_sb, 1)
            a.activation(ra[:, 0:960], probT[:, 0:960], ACT.Copy).then_inc(xch_done, 1)
            act.wait_ge(dup_ps, 2)
            for u in range(2):
                a.activation(kT[u][:, :, :], ps[:, (4, 6)[u], :].rearrange("p (g t) -> p g t", g=2),
                             ACT.Copy).then_inc(proj_sb, 1)
            act.wait_ge(gates_ps, 2)
            a.activation(gates[:, :, :], ps[:, 0, 0:T * GATES].rearrange("p (t n) -> p t n", t=T),
                         ACT.Copy).then_inc(proj_sb, 1)
            split_hi(12)
            for kv in range(2):
                act.wait_ge(unit_used, U_CW1 + 2 * kv + 2)
                a.activation(hnat[0:NG, kv, :], ps[0:NG, HIDDEN[kv], 0:CMP_HID], ACT.Copy).then_inc(hn_sb, 1)
                if kv == 0:
                    split_hi(13)
            for kv in range(2):
                act.wait_ge(hcT_ps, kv + 1)
                for h in range(2):
                    b1 = V_B1 + 2 * kv + h
                    a.activation(hc[:, kv, h, :], ps[:, (2, 6)[kv], h * NG:h * NG + NG], ACT.Gelu_apprx_tanh,
                                 bias=vec[:, b1:b1 + 1]).then_inc(hc_sb, 1)
            act.wait_ge(kv_ps, 1)
            a.activation(kcT[:, :], ps[:, 5, 0:NG], ACT.Identity, bias=vec[:, V_B2K:V_B2K + 1]).then_inc(kc_sb, 1)
            split_hi(14)
            act.wait_ge(sc_sb, 1)
            a.activation(prob[:, 0:240], prob[:, 0:240], ACT.Exp).then_inc(ex_sb, 1)
            for b in range(4):
                act.wait_ge(pcT_ps, b + 1)
                a.activation(pcT[0:NCMP, 4 * b:4 * b + 4, :], ps[0:NCMP, 4 + b, :].rearrange("p (q t) -> p q t", q=4),
                             ACT.Copy).then_inc(pcT_sb, 1)
            split_hi(15)
            def att_exp(m):
                nk = P * (m % 2 + 1)
                pr = prob[:, (m % 2) * 1024:(m % 2) * 1024 + 4 * nk].rearrange("p (h k) -> p h k", h=4)
                act.wait_ge(s_sb, m + 1)
                for h in range(4):
                    ins = a.activation(pr[:, h, :], pr[:, h, :], ACT.Exp, bias=st[:, 16 + 4 * (m % 2) + h:17 + 4 * (m % 2) + h],
                                       accum_out=st[:, 24 + 4 * (m % 2) + h:25 + 4 * (m % 2) + h])
                ins.then_inc(p_sb, 1)

            att_exp(0)
            att_exp(1)
            for m in range(8):
                act.wait_ge(pT_ps, m + 1)
                for b in range(m % 2 + 1):
                    ins = a.activation(probT[:, 512 * b:512 * b + 512], ps[:, 4 + b, :], ACT.Copy)
                ins.then_inc(pT_sb, 1)
                if 1 <= m < 7:
                    att_exp(m + 1)
            for b in range(2):
                act.wait_ge(oT_ps, b + 1)
                a.activation(uT_h[:, 2 * b:2 * b + 2, :], ps[:, 4 + b, :].rearrange("p (c t) -> p c t", c=2),
                             ACT.Copy).then_inc(mh_done, 1)
            for t in range(2):
                act.wait_ge(cnT_ps, t + 1)
                for cc in (2 * t, 2 * t + 1):
                    a.activation(y2[:, cc, :], ps[:, 6 + t, (cc % 2) * S:(cc % 2) * S + S], ACT.Silu,
                                 bias=vec[:, V_CLB + cc:V_CLB + cc + 1],
                                 scale=vec[:, V_CG + cc:V_CG + cc + 1]).then_inc(act_chain, 1)
                    ch.n += 1
                ch.wait()
                a.activation(uT_h[:, 4 + 2 * t:6 + 2 * t, :], y2[:, 2 * t:2 * t + 2, :], ACT.Copy).then_inc(mh_done, 1)
            split_hi(16)
            split_hi(17)
            split_hi(18)
            post_norm(0, U_FFN)

            pre_norm(1, 19, [(gpost[:, :], norm_ffn_post[0:1, :].partition_broadcast(P), post_in)])

            def ffn_silu(b):
                for t in range(T):
                    a.activation(sg[:, t * 256:t * 256 + 256], ps[:, 4 + t, 0:256], ACT.Silu).then_inc(sg_done, 1)

            def ffn_hT(b):
                act.wait_ge(hT_ps, b + 1)
                a.activation(ht[:, 0, 0:512], ps[:, 6, :], ACT.Copy).then_inc(hh_done, 1)

            split_hi(20)
            act.wait_ge(unit_used, 19)
            ffn_silu(0)
            ffn_hT(0)

            def ffn_block(b, k0, it=0):
                split_hi(k0 + 2, it)
                split_hi(k0 + 3, it)
                act.wait_ge(unit_used, k0 + 2 + 9 * it)
                ffn_silu(b)
                split_hi(k0 + 4, it)
                ffn_hT(b)

            ffn_block(1, 19)
            with act.Fori(0, 2) as it:
                for j in range(3):
                    ffn_block(it * 3 + (2 + j), U_FFN + 5 + 3 * j, it)
            for b in range(8, FFN_BLOCKS):
                ffn_block(b, 16 + 3 * b)
            split_hi(51)
            post_norm(1, U_GM)

            pre_norm(2, 52, [(ws[:, :, :], gmlp_w_s[0].rearrange("g t s -> t g s"), ws_in),
                             (gpost[:, :], norm_mix_post[1:2, :].partition_broadcast(P), post_in),
                             (ln_g, gmlp_ln_g.partition_broadcast(P), gm_in),
                             (ln_b, gmlp_ln_b.partition_broadcast(P), gm_in),
                             (router[:, :].rearrange("p (c e) -> p c e", c=KC),
                              moe_w_router[0].rearrange("(c p) e -> p c e", p=P), router_in)])
            for cb in range(4):
                k = U_GM + 2 * cb
                split_hi(k + 3)
                if cb == 0:
                    for b in range(2):
                        act.wait_ge(wsT_ps, b + 1)
                        a.activation(wsT[:, 4 * b:4 * b + 4, :], ps[:, b, :].rearrange("p (g t) -> p g t", g=4),
                                     ACT.Copy).then_inc(wsT_sb, 1)
                    act.wait_ge(router_in, 16)
                    a.activation(ht[:, 0, 0:KC * NE], router[:, :], ACT.Copy).then_inc(wr_hi, 1)
                act.wait_ge(unit_used, k + 2)
                z = z2 if cb < 2 else z1
                for t in range(T):
                    a.activation(z[:, t, (cb % 2) * 512:(cb % 2) * 512 + 512], ps[:, 4 + 2 * (cb % 2) + t, :],
                                 ACT.Gelu_apprx_tanh).then_inc(z_sb, 1)
                if cb < 3:
                    split_hi(k + 4)
            for b in range(4):
                act.wait_ge(gyT_ps, b + 1)
                a.activation(uT_h[:, 2 * b:2 * b + 2, :], ps[:, 4 + b, :].rearrange("p (c t) -> p c t", c=2),
                             ACT.Copy).then_inc(gh_done, 1)
            split_hi(60)
            split_hi(61)
            post_norm(2, U_MOE)

            pre_norm(3)
            act.wait_ge(lg_ps, 1)
            act.wait_ge(route_consts, 4)
            a.activation(lgT[0:NE, :], ps[0:NE, 4, 0:S], ACT.Copy).then_inc(lgT_sb, 1)
            act.wait_ge(ex_in, 1)
            a.activation(st[:, 42:44], st[:, 40:42], ACT.Exp).then_inc(ex_out, 1)

            def y_hi(e, nt):
                act.wait_ge(unit_used, U_MOE + MOE_UNITS * (e + 1))
                for i in range(nt):
                    for q in range(2):
                        ins = a.activation(y_part(0, i, q), ps[:, 2 * i + q, :], ACT.Copy)
                        if i == nt - 1:
                            ins.then_inc(yh_done[q], 1)

            def gather_hi(e, tiles):
                gf = V_FFN + KC
                act.wait_ge(gath_ps, e + 1)
                if len(tiles) == 2:
                    act.wait_ge(comb_ps[3], e)
                w = len(tiles) * P
                for c in range(KC):
                    for i, packed in enumerate(tiles):
                        dst = x_part(0, i, c, packed)
                        bank, o = 4 + c * w // 512, c * w % 512 + i * P
                        ins = a.activation(dst, ps[:, bank, o:o + dst.shape[-1]], ACT.Copy,
                                           scale=vec[:, gf + c:gf + c + 1])
                    if c % 4 == 3:
                        ins.then_inc(xgh_done, 1)

            def blocks(e, j, it, tiles):
                nt = len(tiles)
                act.wait_ge(pt_ps, e + 1)
                a.activation(pt01[:, 0:nt, :], ps[:, 4, 0:nt * S].rearrange("p (i t) -> p i t", i=nt),
                             ACT.Copy).then_inc(pt_sb, 1)
                m0 = MOE_UNITS * j

                def silu(b):
                    g_b = 3 if b == 0 else 6 * b + 1
                    act.wait_ge(unit_used, U_MOE + g_b + 1 + MOE_UNITS * e)
                    i = len(tiles) - 1
                    if tiles[i]:
                        for dst, bank in ((eh, 5 + 2 * i), (esg, 4 + 2 * i)):
                            ins = a.activation(dst[0:HALF, i, :], ps[HALF:P, bank, :], ACT.Copy)
                        ins.then_inc(msg_done, 1)
                    for i, packed in enumerate(tiles):
                        if packed:
                            act.wait_ge(mh_ok, 2 * (MOE_BLOCKS * e + b) + 1)
                            ins = a.activation(esg[0:HALF, i, :], esg[0:HALF, i, :], ACT.Silu)
                        else:
                            ins = a.activation(esg[:, i, :], ps[:, gate_bank(b, i, nt), :], ACT.Silu)
                    ins.then_inc(msg_done, 1 if packed else 2)

                def hT(b):
                    act.wait_ge(mhT_ps, MOE_BLOCKS * e + (b + 1))
                    for i, packed in enumerate(tiles):
                        dst, src = ht[:, 0, 512 * i:512 * i + 512], ps[:, gate_bank(b, i, nt), :]
                        if packed:
                            dst, src = (halves(x_)[:, :, 0, :] for x_ in (dst, src))
                        ins = a.activation(dst, src, ACT.Copy)
                    ins.then_inc(mhh_done, 1)

                a.activation(warm[:, :], neg_half[:, 0:1], ACT.Silu)
                for m in range(3, 6):
                    moe_hi(m0 + m, it)
                silu(0)
                if nt == 1:
                    moe_hi(m0 + 6, it)
                    moe_hi(m0 + 7, it)
                hT(0)
                for b in range(1, MOE_BLOCKS):
                    k = 4 + 6 * (b - 1)
                    for m in range(k + 2, k + 6):
                        if nt == 2 or m > 7:
                            moe_hi(m0 + m, it)
                    silu(b)
                    moe_hi(m0 + k + 6, it)
                    moe_hi(m0 + k + 7, it)
                    hT(b)

            with act.Fori(0, NE // 2) as it:
                for j in range(2):
                    e = 2 * it + j
                    moe_hi(MOE_UNITS * j, it)
                    moe_hi(MOE_UNITS * j + 1, it)
                    act.wait_ge(routed, 1)
                    last = act.value_load(flag[0:1, bass.ds(e + NE, 1)], min_val=0, max_val=2)
                    for nt in (1, 2):
                        with act.If(last == nt):
                            y_hi(e - 1, nt)
                    kind = act.value_load(flag[0:1, bass.ds(e, 1)], min_val=0, max_val=len(KINDS) - 1)
                    for n, tiles in enumerate(KINDS):
                        with act.If(kind == n):
                            gather_hi(e, tiles)
                            moe_hi(MOE_UNITS * j + 2, it)
                            blocks(e, j, it, tiles)
            act.wait_ge(pt_ps, NE)
            act.dma_start(gfin, norm_ffn_post[1:2, :].partition_broadcast(P)).then_inc(post_in, 16)
            last = act.value_load(flag[0:1, 2 * NE:2 * NE + 1], min_val=0, max_val=2)
            for nt in (1, 2):
                with act.If(last == nt):
                    y_hi(NE - 1, nt)
            post_norm(3)

        @block.vector
        def _(dve):
            v = nc.vector
            ch = Chain(dve, dve_chain)
            link = ch.link
            rs_n = [0]

            def split_lo(k, it=0):
                dve.wait_ge(hi_done, k + 1 + 9 * it)
                v.tensor_tensor(w_lo[:, k % PARTS, :], raw[:, raw_slot(k), :],
                                w_hi[:, k % PARTS, :].bitcast(F32), ALU.subtract).then_inc(lo_done, 1)

            def moe_lo(m, it):
                dve.wait_ge(hi_done, U_MOE + m + 1 + 2 * MOE_UNITS * it)
                s = (U_MOE + m) % PARTS
                v.tensor_tensor(w_lo[:, s, :], raw[:, moe_slot(m), :], w_hi[:, s, :].bitcast(F32),
                                ALU.subtract).then_inc(lo_done, 1)

            def rsqrt(dst, src, scale):
                v.tensor_scalar(dst, src, scale, EPS, ALU.mult, ALU.add).then_inc(rs_in, 1)
                rs_n[0] += 1
                dve.wait_ge(rs_out, rs_n[0])

            def pre_norm(n, k=None):
                for t in range(T):
                    dve.wait_ge(ss_done, 2 * n + t + 1)
                    rsqrt(st[:, 2 + t:3 + t], st[:, t:t + 1], 1.0 / D)
                    v.tensor_scalar(xn[:, t, :], xres[:, t, :], st[:, 2 + t:3 + t], None, ALU.mult).then_inc(xn_done, 1)
                if k is not None:
                    split_lo(k)
                g0 = (V_MIX, V_FFN)[n % 2] + KC * (n // 2)
                for c in range(KC):
                    if c % 2 == 0:
                        dve.wait_ge(uh_done, 4 * n + c // 2 + 1)
                    ins = v.scalar_tensor_tensor(out=uT_l[:, c, :], in0=ps[:, c // 2, (c % 2) * S:(c % 2) * S + S],
                                                 scalar=vec[:, g0 + c:g0 + c + 1], in1=uT_h[:, c, :].bitcast(F32),
                                                 op0=ALU.mult, op1=ALU.subtract)
                    if c % 2:
                        ins.then_inc(ul_done, 1)

            def post_norm(n):
                dve.wait_ge(post_in, 16 * (n + 1))
                for t in range(T):
                    dve.wait_ge(pss_done, 2 * n + t + 1)
                    rsqrt(st[:, 6 + t:7 + t], st[:, 4 + t:5 + t], 1.0 / D)
                    if n < 3:
                        src = ps[:, 2 * t:2 * t + 2, :]
                        dst = xn[:, t, :].rearrange("p (h n) -> p h n", h=2)
                        g = gpost[:, :].rearrange("p (h n) -> p h n", h=2)
                    else:
                        src, dst, g = acc[:, t, :], xn[:, t, :], gfin
                    link(v.scalar_tensor_tensor(out=dst, in0=src, scalar=st[:, 6 + t:7 + t],
                                                in1=g, op0=ALU.mult, op1=ALU.mult))
                    v.tensor_tensor(xres[:, t, :], xres[:, t, :], xn[:, t, :], ALU.add).then_inc(x_new, 1)

            dve.wait_ge(vec_ps, 1)
            v.tensor_copy(vec[:, :], ps[:, 7, 0:V_ROWS]).then_inc(vec_sb, 1)
            v.tensor_copy(cw, ps[:, 7, P:P + CC * CONV_W]).then_inc(vec_sb, 1)
            pre_norm(0, 0)
            def glu(i):
                dve.wait_ge(glu_sig, i + 1)
                v.tensor_tensor(cT[:, 2 * i:2 * i + 2, CONV_W - 1:PADT],
                                ps[:, (4, 6)[i], :].rearrange("p (c t) -> p c t", c=2),
                                yT[:, 2 * i:2 * i + 2, :], ALU.mult).then_inc(glu_sb, 1)

            def conv_steps(lo, hi):
                for s_ in range(lo, hi):
                    ch.wait()
                    if s_ == 0 or s_ == LATE:
                        dve.wait_ge(glu_sb, 1 if s_ == 0 else 2)
                    for cc, j in ((0, s_), (1, s_), (2, s_ - LATE)):
                        if not 0 <= j < CONV_W:
                            continue
                        w = cw[:, j * CC + cc:j * CC + cc + 1]
                        if j == 0:
                            ins = v.tensor_scalar(yT[:, cc, :], cT[:, cc, 0:S], w,
                                                  vec[:, V_CB + cc:V_CB + cc + 1], ALU.mult, ALU.add)
                        else:
                            ins = v.scalar_tensor_tensor(out=yT[:, cc, :], in0=cT[:, cc, j:j + S], scalar=w,
                                                         in1=yT[:, cc, :], op0=ALU.mult, op1=ALU.add)
                        ch.add(ins)

            def compressor_input():
                dve.wait_ge(dup_ps, 1)
                for kv in range(2):
                    for g in range(2):
                        for r in range(2):
                            pr = slice(HD * r, HD * r + HD)
                            src = ps[pr, (4, 6)[kv], g * S:g * S + S].rearrange("p (m i) -> p m i", i=CMP_STRIDE)
                            for h in range(2):
                                dst = xcmp[pr, kv, 8 * h:8 * h + 8, g, :]
                                pe = vec[pr, V_PE + 16 * kv + 8 * h:V_PE + 16 * kv + 8 * h + 8]
                                last = v.tensor_tensor(
                                    dst, src[:, h:h + NCMP, r:CMP_STRIDE:2].rearrange("p n c -> p c n"),
                                    pe.unsqueeze(2).to_broadcast([HD, 8, NCMP]), ALU.add)
                last.then_inc(xcmp_sb, 1)

            LATE = 8
            for k in range(1, 4):
                split_lo(k)
            dve.wait_ge(wg_hi, 1)
            v.tensor_tensor(ht[:, 1, 0:KC * GATES], wgate, ht[:, 0, 0:KC * GATES].bitcast(F32),
                            ALU.subtract).then_inc(wg_lo, 1)
            split_lo(4)
            glu(0)
            split_lo(5)
            conv_steps(0, 4)
            split_lo(6)
            glu(1)
            conv_steps(4, 6)
            split_lo(7)
            conv_steps(6, 9)
            split_lo(8)
            compressor_input()
            split_lo(9)
            conv_steps(9, 12)
            split_lo(10)
            conv_steps(12, 15)
            split_lo(11)
            dve.wait_ge(xch_done, 1)
            v.tensor_tensor(ra[:, 1024:1984], probT[:, 0:960], ra[:, 0:960].bitcast(F32),
                            ALU.subtract).then_inc(xcl_done, 1)
            conv_steps(15, 18)
            split_lo(12)
            conv_steps(18, 21)
            split_lo(13)
            conv_steps(21, 24)
            conv_steps(24, 29)
            dve.wait_ge(kv_ps, 2)
            v.tensor_tensor(vc[0:NCMP, :, :], ps[0:NCMP, 4, 0:2 * HD].rearrange("p (g d) -> p g d", g=2),
                            b2v[0:NCMP, :].unsqueeze(1).to_broadcast([NCMP, 2, HD]), ALU.add).then_inc(vc_sb, 1)

            pc = prob[:, 0:240].rearrange("p (f i q n) -> p f i q n", f=2, i=2, q=4)
            dve.wait_ge(sc_ps, 1)
            dve.wait_ge(consts, 4)
            for i in range(2):
                ch.add(v.tensor_tensor(pc[:, :, i, :, :],
                                       ps[:, 0:2, i * 60:i * 60 + 60].rearrange("p f (q n) -> p f q n", q=4),
                                       cadd[:, i, :].unsqueeze(1).unsqueeze(1).to_broadcast([P, 2, 4, NCMP]), ALU.add))
            ch.wait()
            pq = prob[:, 0:240].rearrange("p (q n) -> p q n", n=NCMP)
            link(v.tensor_reduce(st[:, 44:60], pq, AX.X, ALU.max))
            v.tensor_tensor(pq, pq, st[:, 44:60].unsqueeze(2).to_broadcast([P, 16, NCMP]),
                            ALU.subtract).then_inc(sc_sb, 1)
            dve.wait_ge(ex_sb, 1)
            link(v.tensor_reduce(st[:, 44:60], pq, AX.X, ALU.add))
            link(v.reciprocal(st[:, 44:60], st[:, 44:60]))
            coef = st[:, 44:60].rearrange("p (f i q) -> p f i q", f=2, i=2)
            dve.wait_ge(proj_sb, 8)
            for i in range(2):
                for f in range(2):
                    gv = gates[:, i, :].rearrange("p (q f k) -> p q f k", q=4, f=2)[:, :, f, 0]
                    ch.add(v.tensor_tensor(coef[:, f, i, :], coef[:, f, i, :], gv, ALU.mult))
                last = v.tensor_tensor(pc[:, :, i, :, :], pc[:, :, i, :, :],
                                       cmul[:, i, :].unsqueeze(1).unsqueeze(1).to_broadcast([P, 2, 4, NCMP]), ALU.mult)
                ch.add(last)
            ch.wait()
            v.tensor_copy(atmp[:, 0:240], prob[:, 0:240]).then_inc(pc_sb, 1)
            split_lo(14)
            conv_steps(29, CONV_W)
            split_lo(15)
            for i in range(2):
                dve.wait_ge(oc_ps, i + 1)
                v.tensor_tensor(oacc[:, i, :].rearrange("p (q f d) -> p q f d", q=4, f=2),
                                ps[:, 2 + i, :].rearrange("p (q f d) -> p q f d", q=4, f=2),
                                coef[:, :, i, :].rearrange("p f q -> p q f").unsqueeze(3).to_broadcast([P, 4, 2, HD]),
                                ALU.mult).then_inc(oc_sb, 1)

            def att_scores(m):
                i = m % 2
                nk = P * (i + 1)
                pr = prob[:, i * 1024:i * 1024 + 4 * nk]
                mx = st[:, 16 + 4 * i:20 + 4 * i]
                dve.wait_ge(s_ps, m + 1)
                if m < 2:
                    dve.wait_ge(oc_ps, 2)
                link(v.tensor_tensor(pr.rearrange("p (f j k) -> p f j k", f=2, j=2),
                                     ps[:, 2 * i:2 * i + 2, 0:2 * nk].rearrange("p f (j k) -> p f j k", j=2),
                                     mask[:, S - nk:S].unsqueeze(1).unsqueeze(1).to_broadcast([P, 2, 2, nk]), ALU.add))
                link(v.tensor_reduce(mx, pr.rearrange("p (h k) -> p h k", h=4), AX.X, ALU.max))
                v.tensor_scalar(mx, mx, -1.0, None, ALU.mult).then_inc(s_sb, 1)

            def att_coef(m):
                br, g, i = m // 4, m // 2 % 2, m % 2
                dve.wait_ge(p_sb, m + 1)
                cf = st[:, 32 + 4 * i:36 + 4 * i]
                link(v.reciprocal(cf, st[:, 24 + 4 * i:28 + 4 * i]))
                gv = gates[:, i, 12 * g:12 * g + 12].rearrange("p (j f k) -> p f j k", j=2, f=2)[:, :, :, 1 + br]
                link(v.tensor_tensor(cf.rearrange("p (f j) -> p f j", f=2), cf.rearrange("p (f j) -> p f j", f=2),
                                     gv, ALU.mult))

            def att_out(m):
                g, i = m // 2 % 2, m % 2
                cf = st[:, 32 + 4 * i:36 + 4 * i]
                dve.wait_ge(o_ps, m + 1)
                link(v.tensor_tensor(atmp.rearrange("p (j f d) -> p j f d", j=2, f=2),
                                     ps[:, 6 + i, 0:256].rearrange("p (j f d) -> p j f d", j=2, f=2),
                                     cf.rearrange("p (f j) -> p j f", f=2).unsqueeze(3).to_broadcast([P, 2, 2, HD]),
                                     ALU.mult))
                link(v.tensor_tensor(oacc[:, i, g * 256:g * 256 + 256], oacc[:, i, g * 256:g * 256 + 256],
                                     atmp, ALU.add))
                v.tensor_copy(st[:, 60:61], cf[:, 0:1]).then_inc(o_sb, 1)

            att_scores(0)
            att_scores(1)
            for m in range(8):
                att_coef(m)
                if m < 6:
                    att_scores(m + 2)
                conv_steps(CONV_W + m, CONV_W + m + 1)
                if m == LATE - 1:
                    ch.wait()
                    v.tensor_copy(st[:, 61:62], yT[:, 2, 0:1]).then_inc(conv_vec, 1)
                att_out(m)

            for b in range(2):
                dve.wait_ge(mh_done, 1 + b)
                v.tensor_tensor(uT_l[:, 2 * b:2 * b + 2, :], ps[:, 4 + b, :].rearrange("p (c t) -> p c t", c=2),
                                uT_h[:, 2 * b:2 * b + 2, :].bitcast(F32), ALU.subtract).then_inc(ml_done, 1)
            for t in range(T):
                o = 64 + 8 * t
                dve.wait_ge(cn_ps, t + 1)
                link(v.bn_stats(st[:, o:o + 6], ps[:, 6 + t, :]))
                link(v.bn_aggr(st[:, o + 6:o + 8], st[:, o:o + 6]))
                rsqrt(st[:, o + 7:o + 8], st[:, o + 7:o + 8], 1.0)
                v.tensor_scalar(cn[:, t, :], ps[:, 6 + t, :], st[:, o + 6:o + 7], st[:, o + 7:o + 8],
                                ALU.subtract, ALU.mult).then_inc(cn_sb, 1)
            for t in range(2):
                dve.wait_ge(mh_done, t + 3)
                v.tensor_tensor(uT_l[:, 4 + 2 * t:6 + 2 * t, :], y2[:, 2 * t:2 * t + 2, :],
                                uT_h[:, 4 + 2 * t:6 + 2 * t, :].bitcast(F32), ALU.subtract).then_inc(ml_done, 1)
            split_lo(16)
            split_lo(17)
            split_lo(18)
            post_norm(0)

            pre_norm(1, 19)

            def ffn_h(b):
                for t in range(T):
                    dve.wait_ge(sg_done, 2 * b + (t + 1))
                    v.tensor_tensor(hbuf[:, t * 256:t * 256 + 256], sg[:, t * 256:t * 256 + 256],
                                    ps[:, 4 + t, 256:512], ALU.mult).then_inc(h_done, 1)

            def ffn_hT(b):
                dve.wait_ge(hh_done, b + 1)
                v.tensor_tensor(ht[:, 1, 0:512], ps[:, 6, :], ht[:, 0, 0:512].bitcast(F32), ALU.subtract).then_inc(hl_done, 1)

            def ffn_block(b, k0, it=0):
                split_lo(k0 + 2, it)
                split_lo(k0 + 3, it)
                ffn_h(b)
                split_lo(k0 + 4, it)
                ffn_hT(b)

            split_lo(20)
            ffn_h(0)
            ffn_hT(0)
            ffn_block(1, 19)
            with dve.Fori(0, 2) as it:
                for j in range(3):
                    ffn_block(it * 3 + (2 + j), U_FFN + 5 + 3 * j, it)
            for b in range(8, FFN_BLOCKS):
                ffn_block(b, 16 + 3 * b)
            split_lo(51)
            post_norm(1)

            pre_norm(2, 52)
            def gate_z(h):
                dve.wait_ge(z_sb, 6 + 2 * h)
                for t in range(T):
                    dve.wait_ge(mixed_ps, 2 * t + h + 1)
                    for g in range(4 * h, 4 * h + 4):
                        last = v.scalar_tensor_tensor(
                            out=z1[:, t, g * P:g * P + P], in0=ps[:, 2 * t + h, (g % 4) * P:(g % 4) * P + P],
                            scalar=vec[:, V_BS + g:V_BS + g + 1], in1=z1[:, t, g * P:g * P + P],
                            op0=ALU.add, op1=ALU.mult)
                    last.then_inc(gy_done, 1)

            for cb in range(4):
                k = U_GM + 2 * cb
                split_lo(k + 3)
                if cb < 3:
                    split_lo(k + 4)
                if cb >= 2:
                    gate_z(cb - 2)
                if cb == 3:
                    dve.wait_ge(wr_hi, 1)
                    v.tensor_tensor(ht[:, 1, 0:KC * NE], router[:, :], ht[:, 0, 0:KC * NE].bitcast(F32),
                                    ALU.subtract).then_inc(wr_lo, 1)
                if cb == 1:
                    dve.wait_ge(gm_in, 32)
                    dve.wait_ge(z_sb, 4)
                    for t in range(T):
                        for h in range(2):
                            ch.add(v.bn_stats(st[:, 44 + 6 * h:50 + 6 * h], z2[:, t, h * 512:h * 512 + 512]))
                        ch.wait()
                        link(v.bn_aggr(st[:, 56:58], st[:, 44:56].rearrange("p (h s) -> p h s", h=2)))
                        rsqrt(st[:, 57:58], st[:, 57:58], 1.0)
                        link(v.scalar_tensor_tensor(out=z2[:, t, :], in0=z2[:, t, :], scalar=st[:, 56:57],
                                                    in1=ln_g, op0=ALU.subtract, op1=ALU.mult))
                        v.scalar_tensor_tensor(out=z2[:, t, :], in0=z2[:, t, :], scalar=st[:, 57:58],
                                               in1=ln_b, op0=ALU.mult, op1=ALU.add).then_inc(z2_done, 1)
            for b in range(4):
                dve.wait_ge(gh_done, b + 1)
                v.tensor_tensor(uT_l[:, 2 * b:2 * b + 2, :], ps[:, 4 + b, :].rearrange("p (c t) -> p c t", c=2),
                                uT_h[:, 2 * b:2 * b + 2, :].bitcast(F32), ALU.subtract).then_inc(gl_done, 1)
            split_lo(60)
            split_lo(61)
            post_norm(2)

            pre_norm(3)

            def small(i):
                return rt[:, 16 * i:16 * i + 16].rearrange("p (t e) -> p t e", t=T)

            lg, eq, mk1, mk2, io8, mm, _, mr, pos, cnt = (small(i) for i in range(10))
            col = rt[:, 160:176]
            w_out = rt[:, 192:210].rearrange("p (t e) -> p t e", t=T)

            def over(c):
                return c.unsqueeze(2).to_broadcast([P, T, NE])

            v.memset(acc[:, :, :], 0.0).then_inc(dve_chain, 1)
            ch.n += 1
            dve.wait_ge(route_consts, 4)
            link(v.tensor_scalar(io8, iota[:, 0:NE].unsqueeze(1).to_broadcast([P, T, NE]), float(-NE), None, ALU.add))
            dve.wait_ge(lg_ps, 2)
            link(v.tensor_copy(lg, ps[:, 6, 0:T * NE].rearrange("p (t e) -> p t e", t=T)))

            def top(mx, idx, mk):
                link(v.tensor_reduce(mx, lg, AX.X, ALU.max))
                link(v.tensor_tensor(eq, lg, over(mx), ALU.is_equal))
                link(v.tensor_tensor(eq, eq, io8, ALU.mult))
                link(v.tensor_reduce(idx, eq, AX.X, ALU.min))
                link(v.tensor_tensor(mk, io8, over(idx), ALU.is_equal))

            top(col[:, 0:2], col[:, 4:6], mk1)
            link(v.scalar_tensor_tensor(out=lg, in0=mk1, scalar=-3e38, in1=lg, op0=ALU.mult, op1=ALU.add))
            top(col[:, 2:4], col[:, 4:6], mk2)
            v.tensor_tensor(st[:, 40:42], col[:, 2:4], col[:, 0:2], ALU.subtract).then_inc(ex_in, 1)
            link(v.tensor_tensor(mm, mk1, mk2, ALU.add))
            link(v.tensor_tensor(mr, mm, over(st[:, 2:4]), ALU.mult))
            v.tensor_copy(eq, mm).then_inc(m_done, 1)
            dve.wait_ge(ex_out, 1)
            link(v.tensor_scalar(col[:, 0:2], st[:, 42:44], 1.0, None, ALU.add))
            link(v.reciprocal(col[:, 0:2], col[:, 0:2]))
            link(v.tensor_tensor(col[:, 2:4], col[:, 0:2], st[:, 42:44], ALU.mult))
            link(v.tensor_tensor(mk1, mk1, over(col[:, 0:2]), ALU.mult))
            link(v.tensor_tensor(mk2, mk2, over(col[:, 2:4]), ALU.mult))
            link(v.memset(w_out, 0.0))
            link(v.tensor_tensor(w_out[:, :, 1:NE + 1], mk1, mk2, ALU.add))
            dve.wait_ge(pos_ps, 1)
            link(v.tensor_copy(pos, ps[:, 5, 0:T * NE].rearrange("p (t e) -> p t e", t=T)))
            kind, last = cnt[:, 0, :], rt[:, 176:176 + NE + 1]
            total = ps[:, 5, T * NE:(T + 1) * NE]
            link(v.memset(last, 0.0))
            ch.add(v.tensor_scalar(last[:, 1:NE + 1], total, float(KIND_LIMITS[0]), 1.0, ALU.is_gt, ALU.add))
            link(v.tensor_scalar(kind, total, float(KIND_LIMITS[0]), None, ALU.is_gt))
            link(v.scalar_tensor_tensor(out=kind, in0=total, scalar=float(KIND_LIMITS[1]), in1=kind,
                                        op0=ALU.is_gt, op1=ALU.add))
            link(v.tensor_copy(flag[:, 0:NE], kind))
            v.tensor_copy(flag[:, NE:2 * NE + 1], last).then_inc(routed, 1)
            dve.wait_ge(routed, 1)

            def select(e, tiles):
                n = len(tiles) * P
                for dst, m in ((selr, mr), (sel01, mm)):
                    for t in range(T):
                        o = n - P if tiles[-1] and dst is sel01 else n
                        at_e = pos[:, t, bass.ds(e, 1)], m[:, t, bass.ds(e, 1)]
                        if o:
                            ins = v.tensor_scalar(dst[:, t, 0:o], iota[:, 0:o], *at_e, ALU.is_equal, ALU.mult)
                        if o < n:
                            ins = v.tensor_scalar(dst[:, t, o:n].rearrange("p (h j) -> p h j", h=2),
                                                  iota[:, o:o + HALF].unsqueeze(1).to_broadcast([P, 2, HALF]),
                                                  *at_e, ALU.is_equal, ALU.mult)
                ins.then_inc(sel_done, 1)

            def y_lo(e, nt):
                for i in range(nt):
                    for q in range(2):
                        if i == 0:
                            dve.wait_ge(yh_done[q], e + 1)
                        ins = v.tensor_tensor(y_part(1, i, q), ps[:, 2 * i + q, :],
                                              y_part(0, i, q).bitcast(F32), ALU.subtract)
                        if i == nt - 1:
                            ins.then_inc(yl_done, 1)

            def gather_lo(e, tiles):
                gf, w = V_FFN + KC, len(tiles) * P
                for c in range(KC):
                    if c % 4 == 0:
                        dve.wait_ge(xgh_done, 2 * e + (c // 4 + 1))
                    for i, packed in enumerate(tiles):
                        hi, dst = (x_part(part, i, c, packed) for part in range(2))
                        bank, o = 4 + c * w // 512, c * w % 512 + i * P
                        ins = v.scalar_tensor_tensor(
                            out=dst, in0=ps[:, bank, o:o + dst.shape[-1]], scalar=vec[:, gf + c:gf + c + 1],
                            in1=hi.bitcast(F32), op0=ALU.mult, op1=ALU.subtract)
                ins.then_inc(xgl_done, 1)

            def add_out(e):
                for t in range(T):
                    for q in range(2):
                        dve.wait_ge(comb_ps[2 * t + q], e + 1)
                        a_ = acc[:, t, q * 512:q * 512 + 512]
                        v.scalar_tensor_tensor(out=a_, in0=ps[:, (2, 0)[t] + q, :], scalar=w_out[:, t, bass.ds(e + 1, 1)],
                                               in1=a_, op0=ALU.mult, op1=ALU.add).then_inc(acc_done, 1)

            def blocks(e, j, it, tiles):
                m0 = MOE_UNITS * j

                def h(b):
                    i = len(tiles) - 1
                    if tiles[i]:
                        dve.wait_ge(msg_done, 2 * (MOE_BLOCKS * e + b) + 1)
                        for dst, bank in ((eh, 5 + 2 * i), (esg, 4 + 2 * i)):
                            ins = v.tensor_tensor(dst[0:HALF, i, :], ps[0:HALF, bank, :], dst[0:HALF, i, :], ALU.add)
                        ins.then_inc(mh_ok, 1)
                    dve.wait_ge(msg_done, 2 * (MOE_BLOCKS * e + (b + 1)))
                    for i, packed in enumerate(tiles):
                        rows = slice(0, HALF if packed else P)
                        up = eh[rows, i, :] if packed else ps[:, gate_bank(b, i, len(tiles)) + 1, :]
                        ins = v.tensor_tensor(eh[rows, i, :], esg[rows, i, :], up, ALU.mult)
                    ins.then_inc(mh_ok, 1 if packed else 2)

                def hT(b):
                    dve.wait_ge(mhh_done, MOE_BLOCKS * e + (b + 1))
                    for i, packed in enumerate(tiles):
                        hi, dst = (ht[:, part, 512 * i:512 * i + 512] for part in range(2))
                        src = ps[:, gate_bank(b, i, len(tiles)), :]
                        if packed:
                            dst, src, hi = halves(hi)[:, :, 1, :], halves(src)[:, :, 0, :], halves(hi)[:, :, 0, :]
                        ins = v.tensor_tensor(dst, src, hi.bitcast(F32), ALU.subtract)
                    ins.then_inc(mhl_done, 1)

                dve.wait_ge(acc_done, 4 * e)
                for m in range(3, 6):
                    moe_lo(m0 + m, it)
                h(0)
                if len(tiles) == 1:
                    moe_lo(m0 + 6, it)
                    moe_lo(m0 + 7, it)
                hT(0)
                for b in range(1, MOE_BLOCKS):
                    k = 4 + 6 * (b - 1)
                    for m in range(k + 2, k + 6):
                        if len(tiles) == 2 or m > 7:
                            moe_lo(m0 + m, it)
                    h(b)
                    moe_lo(m0 + k + 6, it)
                    moe_lo(m0 + k + 7, it)
                    hT(b)

            with dve.Fori(0, NE // 2) as it:
                for j in range(2):
                    e = 2 * it + j
                    kind = dve.value_load(flag[0:1, bass.ds(e, 1)], min_val=0, max_val=len(KINDS) - 1)
                    last_e = dve.value_load(flag[0:1, bass.ds(e + NE, 1)], min_val=0, max_val=2)
                    for n, tiles in enumerate(KINDS):
                        with dve.If(kind == n):
                            select(e, tiles)
                    moe_lo(MOE_UNITS * j, it)
                    moe_lo(MOE_UNITS * j + 1, it)
                    for nt in (1, 2):
                        with dve.If(last_e == nt):
                            y_lo(e - 1, nt)
                    for n, tiles in enumerate(KINDS):
                        with dve.If(kind == n):
                            gather_lo(e, tiles)
                    moe_lo(MOE_UNITS * j + 2, it)
                    with dve.If(last_e > 0):
                        add_out(e - 1)
                    for n, tiles in enumerate(KINDS):
                        with dve.If(kind == n):
                            blocks(e, j, it, tiles)
            last_e = dve.value_load(flag[0:1, 2 * NE:2 * NE + 1], min_val=0, max_val=2)
            for nt in (1, 2):
                with dve.If(last_e == nt):
                    y_lo(NE - 1, nt)
            add_out(NE - 1)
            dve.wait_ge(acc_done, 4 * NE)
            post_norm(3)

        @block.tensor
        def _(pe):
            t_ = nc.tensor

            def mm3(dst, lh, ll, rh, rl, start, stop):
                t_.matmul(dst, lh, rh, start=start, stop=False)
                t_.matmul(dst, lh, rl, start=False, stop=False)
                return t_.matmul(dst, ll, rh, start=False, stop=stop)

            def unit(k, it=0):
                pe.wait_ge(lo_done, k + 1 + 9 * it)
                return w_hi[:, k % PARTS, :], w_lo[:, k % PARTS, :]

            def views(k, c, it=0):
                h, l = unit(k, it)
                return (h.rearrange("p (c n) -> p c n", c=c), l.rearrange("p (c n) -> p c n", c=c))

            def pre_norm(n):
                for t in range(T):
                    pe.wait_ge(xn_done, 2 * n + t + 1)
                    for c in range(KC):
                        last = t_.transpose(ps[:, c // 2, (c % 2) * S + t * P:(c % 2) * S + t * P + P],
                                            xn[:, t, c * P:c * P + P], ident[:, :])
                        if t == T - 1 and c % 2:
                            last.then_inc(xT_ps, 1)

            def by_tile(mm, final):
                if not final:
                    for kk in range(2):
                        for t in range(T):
                            last = mm(kk, t)
                else:
                    for t in range(T):
                        for kk in range(2):
                            last = mm(kk, t)
                        if t == 0:
                            last.then_inc(tile0_ps, 1)
                last.then_inc(unit_used, 1)

            def out_proj(k0, j0, j1):
                for j in range(j0, j1):
                    h, l = views(k0 + j, 2)

                    def mm(kk, t):
                        c = 2 * j + kk
                        for q in range(2):
                            last = mm3(ps[:, 2 * t + q, :], uT_h[:, c, t * P:t * P + P], uT_l[:, c, t * P:t * P + P],
                                       h[:, kk, q * 512:q * 512 + 512], l[:, kk, q * 512:q * 512 + 512],
                                       c == 0, c == KC - 1)
                        return last

                    by_tile(mm, j == 3)

            pe.wait_ge(consts, 1)
            pe.wait_ge(vec_in, 16 * VEC_LOADS)
            t_.transpose(ps[:, 7, 0:V_ROWS], vec_rows[0:V_ROWS, :], ident[0:V_ROWS, 0:V_ROWS])
            t_.transpose(ps[:, 7, P:P + CC * CONV_W], cw_rows[0:CC * CONV_W, :],
                         ident[0:CC * CONV_W, 0:CC * CONV_W]).then_inc(vec_ps, 1)
            pre_norm(0)
            pe.wait_ge(ul_done, 4)

            def cols_proj(dst, h, l, c0):
                for c in range(KC):
                    last = mm3(dst, h[:, c, c0:c0 + P], l[:, c, c0:c0 + P], uT_h[:, c, :], uT_l[:, c, :], c == 0, c == KC - 1)
                return last

            def rows_proj(dst, t, wh, wl):
                for c in range(KC):
                    last = mm3(dst, uT_h[:, c, t * P:t * P + P], uT_l[:, c, t * P:t * P + P],
                               wh(c), wl(c), c == 0, c == KC - 1)
                return last

            for k in range(4):
                h, l = views(U_GLU + k, 8)
                if k == 3:
                    pe.wait_ge(vec_sb, 2)
                for i in range(2):
                    last = cols_proj(ps[:, 4 + k, i * S:i * S + S], h, l, i * P)
                last.then_inc(unit_used, 1)
            h, l = views(U_CMP_IN, 8)
            for kv in range(2):
                last = cols_proj(ps[:, 2, kv * S:kv * S + S], h, l, kv * P)
            last.then_inc(unit_used, 1)
            for u in range(2):
                h, l = views(U_Q + u, 8)
                for j in range(2):
                    last = cols_proj(ps[:, u, j * S:j * S + S], h, l, j * P)
                last.then_inc(unit_used, 1)

            def to_both(dst, k):
                for g in range(2):
                    last = t_.matmul(dst[:, g * S:g * S + S], both[:, g, :], ktmp[:, k, :], start=True, stop=True)
                return last

            pe.wait_ge(consts, 5)
            pe.wait_ge(proj_sb, 1)
            pe.wait_ge(glu_sb, 2)
            to_both(ps[:, 4, :], 0)
            to_both(ps[:, 6, :], 1).then_inc(dup_ps, 1)
            for u in range(2):
                h, l = views(U_SLC + u, 8)
                if u == 0:
                    pe.wait_ge(glu_sig, 2)
                cols_proj(ps[:, (3, 7)[u], 0:S], h, l, 0)
                for t in range(T):
                    last = rows_proj(ps[:, (5, 2)[u], t * P:t * P + P], t,
                                     lambda c: h[:, c, P:2 * P], lambda c: l[:, c, P:2 * P])
                last.then_inc(unit_used, 1)
            pe.wait_ge(wg_lo, 1)
            pe.wait_ge(proj_sb, 2)
            gh, gl = (ht[:, i, 0:KC * GATES].rearrange("p (c n) -> p c n", c=KC) for i in range(2))
            for c in range(KC):
                last = mm3(ps[0:GATES, 0, 0:S], gh[:, c, :], gl[:, c, :], uT_h[:, c, :], uT_l[:, c, :], c == 0, c == KC - 1)
            last.then_inc(gates_ps, 1)
            pe.wait_ge(proj_sb, 7)
            pe.wait_ge(xcmp_sb, 1)
            to_both(ps[:, 4, :], 2)
            to_both(ps[:, 6, :], 3).then_inc(dup_ps, 1)
            pe.wait_ge(gT_sb, 1)
            for t in range(T):
                last = t_.transpose(ps[:, 0, t * GATES:t * GATES + GATES], atmp[0:GATES, t * P:t * P + P],
                                    ident[0:GATES, 0:GATES])
            last.then_inc(gates_ps, 1)

            pe.wait_ge(xcl_done, 1)
            for j in range(4):
                kv = j // 2
                h, l = views(U_CW1 + j, 8)
                for c in range(8):
                    cx = 8 * (j % 2) + c
                    last = mm3(ps[0:NG, HIDDEN[kv], 0:CMP_HID], xc_h[:, kv, cx, :], xc_l[:, kv, cx, :],
                               h[:, c, :], l[:, c, :], cx == 0, cx == 15)
                last.then_inc(unit_used, 1)
            for kv in range(2):
                pe.wait_ge(hn_sb, kv + 1)
                if kv == 1:
                    pe.wait_ge(proj_sb, 9)
                for hh in range(2):
                    last = t_.transpose(ps[:, (2, 6)[kv], hh * NG:hh * NG + NG], hnat[0:NG, kv, hh * P:hh * P + P],
                                        ident[0:NG, 0:NG])
                last.then_inc(hcT_ps, 1)
            pe.wait_ge(hc_sb, 2)
            for hh in range(2):
                last = t_.matmul(ps[:, 5, 0:NG], w2k[:, hh, :], hc[:, 0, hh, :], start=hh == 0, stop=hh == 1)
            last.then_inc(kv_ps, 1)
            pe.wait_ge(hc_sb, 4)
            for g in range(2):
                for hh in range(2):
                    last = t_.matmul(ps[0:NCMP, 4, g * HD:g * HD + HD], hc[:, 1, hh, g * NCMP:g * NCMP + NCMP],
                                     w2v[:, hh, :], start=hh == 0, stop=hh == 1)
            last.then_inc(kv_ps, 1)

            pe.wait_ge(kc_sb, 1)
            pe.wait_ge(proj_sb, 10)
            for i in range(2):
                for g in range(2):
                    for j in range(2):
                        for f in range(2):
                            q = i * 4 + 2 * g + j
                            fs = slice(HD * f, HD * f + HD)
                            last = t_.matmul(ps[:, f, q * NCMP:q * NCMP + NCMP], qT[fs, 2 * g + j, i * P:i * P + P],
                                             kcT[fs, g * NCMP:g * NCMP + NCMP], start=True, stop=True)
            last.then_inc(sc_ps, 1)
            pe.wait_ge(pc_sb, 1)
            pe.wait_ge(vc_sb, 1)
            for q in range(16):
                last = t_.transpose(ps[0:NCMP, 4 + q // 4, (q % 4) * P:(q % 4) * P + P],
                                    atmp[:, q * NCMP:q * NCMP + NCMP], ident[:, :])
                if q % 4 == 3:
                    last.then_inc(pcT_ps, 1)
            def scores(m):
                br, g, i = m // 4, m // 2 % 2, m % 2
                nk = P * (i + 1)
                if m == 0:
                    pe.wait_ge(sc_sb, 1)
                elif m == 1:
                    pe.wait_ge(oc_sb, 2)
                else:
                    pe.wait_ge(s_sb, m - 1)
                for j in range(2):
                    for f in range(2):
                        fs = slice(HD * f, HD * f + HD)
                        last = t_.matmul(ps[:, 2 * i + f, j * nk:j * nk + nk], qT[fs, 2 * g + j, i * P:i * P + P],
                                         kT[br][fs, g, 0:nk], start=True, stop=True)
                last.then_inc(s_ps, 1)

            scores(0)
            pe.wait_ge(pcT_sb, 4)
            for i in range(2):
                for q in range(4):
                    for f in range(2):
                        h = 2 * q + f
                        last = t_.matmul(ps[:, 2 + i, h * HD:h * HD + HD], pcT[0:NCMP, f * 8 + i * 4 + q, :],
                                         vc[0:NCMP, q // 2, :], start=True, stop=True)
                last.then_inc(oc_ps, 1)

            scores(1)
            for m in range(8):
                br, g, i = m // 4, m // 2 % 2, m % 2
                nk = P * (i + 1)
                pr = prob[:, i * 1024:i * 1024 + 4 * nk]
                pe.wait_ge(p_sb, m + 1)
                for s in range(4 * (i + 1)):
                    last = t_.transpose(ps[:, 4 + s // 4, (s % 4) * P:(s % 4) * P + P], pr[:, s * P:s * P + P], ident[:, :])
                last.then_inc(pT_ps, 1)
                if m < 6:
                    scores(m + 2)
                pe.wait_ge(pT_sb, m + 1)
                if m >= 2:
                    pe.wait_ge(o_sb, m - 1)
                for j in range(2):
                    for f in range(2):
                        hh = 2 * j + f
                        for kb in range(i + 1):
                            s = (2 * f + j) * (i + 1) + kb
                            last = t_.matmul(ps[:, 6 + i, hh * HD:hh * HD + HD], probT[:, s * P:s * P + P],
                                             vv[br][:, kb, g * HD:g * HD + HD], start=kb == 0, stop=kb == i)
                last.then_inc(o_ps, 1)

            pe.wait_ge(o_sb, 8)
            for c in range(4):
                for t in range(T):
                    last = t_.transpose(ps[:, 4 + c // 2, (c % 2) * S + t * P:(c % 2) * S + t * P + P],
                                        oacc[:, t, c * P:c * P + P], ident[:, :])
                if c % 2:
                    last.then_inc(oT_ps, 1)
            pe.wait_ge(conv_vec, 1)
            pe.wait_ge(conv_pool, 1)
            for t in range(T):
                for cc in range(CC):
                    last = t_.transpose(ps[:, 6 + t, cc * P:cc * P + P], yT[:, cc, t * P:t * P + P], ident[:, :])
                last.then_inc(cn_ps, 1)
            pe.wait_ge(ml_done, 2)
            out_proj(U_OUT0, 0, 1)
            pe.wait_ge(cn_sb, 2)
            for cc in range(CC):
                for t in range(T):
                    last = t_.transpose(ps[:, 6 + cc // 2, (cc % 2) * S + t * P:(cc % 2) * S + t * P + P],
                                        cn[:, t, cc * P:cc * P + P], ident[:, :])
                if cc % 2:
                    last.then_inc(cnT_ps, 1)
            out_proj(U_OUT0, 1, 2)
            pe.wait_ge(ml_done, 4)
            out_proj(U_OUT0, 2, 4)

            pe.wait_ge(x_new, 2)
            pre_norm(1)

            def ffn_gu(b, k, half, it=0):
                h, l = (w.rearrange("p (c n) -> p c n", c=4) for w in unit(k, it))
                for t in range(T):
                    for cc in range(4):
                        c = 4 * half + cc
                        last = mm3(ps[:, 4 + t, :], uT_h[:, c, t * P:t * P + P], uT_l[:, c, t * P:t * P + P],
                                   h[:, cc, :], l[:, cc, :], c == 0, c == KC - 1)
                last.then_inc(unit_used, 1)

            def ffn_T(b):
                pe.wait_ge(h_done, 2 * b + 2)
                for c in range(2):
                    for t in range(T):
                        last = t_.transpose(ps[:, 6, c * S + t * P:c * S + t * P + P],
                                            hbuf[:, t * 256 + c * P:t * 256 + c * P + P], ident[:, :])
                last.then_inc(hT_ps, 1)

            def ffn_down(b, k, it=0, first=False, final=False):
                h, l = views(k, 2, it)
                pe.wait_ge(hl_done, b + 1)

                def mm(c, t):
                    for q in range(2):
                        last = mm3(ps[:, 2 * t + q, :], ht[:, 0, c * S + t * P:c * S + t * P + P],
                                   ht[:, 1, c * S + t * P:c * S + t * P + P],
                                   h[:, c, q * 512:q * 512 + 512], l[:, c, q * 512:q * 512 + 512],
                                   first and c == 0, final and c == 1)
                    return last

                by_tile(mm, final)

            k = U_FFN
            pe.wait_ge(ul_done, 6)
            ffn_gu(0, k, 0)
            pe.wait_ge(ul_done, 8)
            ffn_gu(0, k + 1, 1)
            ffn_T(0)
            ffn_gu(1, k + 2, 0)
            ffn_gu(1, k + 3, 1)
            ffn_down(0, k + 4, first=True)
            ffn_T(1)
            with pe.Fori(0, 3) as it:
                for j in range(3):
                    k = U_FFN + 5 + 3 * j
                    b = it * 3 + (FFN_LOOP0 + j)
                    ffn_gu(b, k, 0, it)
                    ffn_gu(b, k + 1, 1, it)
                    ffn_down(b - 1, k + 2, it)
                    ffn_T(b)
            ffn_down(FFN_BLOCKS - 1, U_GM - 1, final=True)

            def z_in(cb, a):
                h, l = views(U_GM + 2 * cb + a, 4)
                for t in range(T):
                    for cc in range(4):
                        c = 4 * a + cc
                        last = mm3(ps[:, 4 + 2 * (cb % 2) + t, :], uT_h[:, c, t * P:t * P + P],
                                   uT_l[:, c, t * P:t * P + P], h[:, cc, :], l[:, cc, :], c == 0, c == KC - 1)
                last.then_inc(unit_used, 1)

            pe.wait_ge(x_new, 4)
            pre_norm(2)
            for a in range(2):
                pe.wait_ge(ul_done, 10 + 2 * a)
                z_in(0, a)
            pe.wait_ge(ul_done, 12)
            pe.wait_ge(ws_masked, 1)
            for g in range(8):
                last = t_.transpose(ps[:, g // 4, (g % 4) * P:(g % 4) * P + P], ws[:, g, :], ident[:, :])
                if g % 4 == 3:
                    last.then_inc(wsT_ps, 1)
            for cb in range(1, 4):
                if cb >= 2:
                    pe.wait_ge(z_sb, 2 * (cb - 1))
                if cb == 3:
                    pe.wait_ge(wsT_sb, 2)
                    for t in range(T):
                        pe.wait_ge(z2_done, t + 1)
                        for g in range(8):
                            last = t_.matmul(ps[:, 2 * t + g // 4, (g % 4) * P:(g % 4) * P + P], wsT[:, g, :],
                                             z2[:, t, g * P:g * P + P], start=True, stop=True)
                            if g % 4 == 3:
                                last.then_inc(mixed_ps, 1)
                for a in range(2):
                    z_in(cb, a)
            for h in range(2):
                pe.wait_ge(gy_done, 2 * h + 2)
                for c in range(4 * h, 4 * h + 4):
                    for t in range(T):
                        last = t_.transpose(ps[:, 4 + c // 2, (c % 2) * S + t * P:(c % 2) * S + t * P + P],
                                            z1[:, t, c * P:c * P + P], ident[:, :])
                    if c % 2:
                        last.then_inc(gyT_ps, 1)
            pe.wait_ge(gl_done, 2)
            out_proj(U_GMO, 0, 2)
            pe.wait_ge(gl_done, 4)
            out_proj(U_GMO, 2, 4)

            pe.wait_ge(x_new, 6)
            pre_norm(3)
            pe.wait_ge(ul_done, 16)
            pe.wait_ge(wr_lo, 1)
            rh, rl = (ht[:, i, 0:KC * NE].rearrange("p (c n) -> p c n", c=KC) for i in range(2))
            for c in range(KC):
                last = mm3(ps[0:NE, 4, 0:S], rh[:, c, :], rl[:, c, :], uT_h[:, c, :], uT_l[:, c, :], c == 0, c == KC - 1)
            last.then_inc(lg_ps, 1)
            pe.wait_ge(lgT_sb, 1)
            for t in range(T):
                last = t_.transpose(ps[:, 6, t * NE:t * NE + NE], lgT[0:NE, t * P:t * P + P], ident[0:NE, 0:NE])
            last.then_inc(lg_ps, 1)
            pe.wait_ge(m_done, 1)
            pe.wait_ge(route_consts, 4)
            mk = rt[:, 80:96].rearrange("p (t e) -> p t e", t=T)
            t_.matmul(ps[:, 5, 0:NE], tri[:, :], mk[:, 0, :], start=True, stop=True)
            t_.matmul(ps[:, 5, NE:2 * NE], tri[:, :], mk[:, 1, :], start=True, stop=False)
            t_.matmul(ps[:, 5, NE:2 * NE], ones[:, :], mk[:, 0, :], start=False, stop=True)
            t_.matmul(ps[:, 5, 2 * NE:3 * NE], ones[:, :], mk[:, 0, :], start=True, stop=False)
            t_.matmul(ps[:, 5, 2 * NE:3 * NE], ones[:, :], mk[:, 1, :], start=False, stop=True).then_inc(pos_ps, 1)

            def gather(e, nt):
                w = nt * P
                pe.wait_ge(sel_done, e + 1)
                for c in range(KC):
                    bank, o = 4 + c * w // 512, c * w % 512
                    for t in range(T):
                        last = t_.matmul(ps[:, bank, o:o + w], xres[:, t, c * P:c * P + P],
                                         selr[:, t, 0:w], start=t == 0, stop=t == 1)
                last.then_inc(gath_ps, 1)

            def combine(e, nt):
                pe.wait_ge(pt_sb, e + 1)
                pe.wait_ge(yl_done, 2 * e + 2)
                for t in range(T):
                    for q in range(2):
                        for i in range(nt):
                            for part in range(2):
                                last = t_.matmul(ps[:, (2, 0)[t] + q, :], pt01[:, i, t * P:t * P + P],
                                                 y_part(part, i, q), start=i + part == 0,
                                                 stop=i == nt - 1 and part == 1)
                        last.then_inc(comb_ps[2 * t + q], 1)

            def mm_tile(dst, lhs, rh, rl, packed, start, stop):
                if not packed:
                    return mm3(dst, lhs(0), lhs(1), rh, rl, start, stop)
                both_, hi = lhs(0), lhs(0)[:, 0:HALF]
                if not stop:
                    t_.matmul(dst, both_, rh, start=start, stop=False)
                    return t_.matmul(dst[0:HALF], hi, rl, start=False, stop=False)
                t_.matmul(dst[0:HALF], hi, rl, start=False, stop=False)
                return t_.matmul(dst, both_, rh, start=False, stop=True)

            def blocks(e, j, it, tiles):
                nt = len(tiles)
                pe.wait_ge(xgl_done, e + 1)
                for i in range(nt):
                    for t in range(T):
                        last = t_.transpose(ps[:, 4, i * S + t * P:i * S + t * P + P],
                                            sel01[:, t, i * P:i * P + P], ident[:, :])
                last.then_inc(pt_ps, 1)

                def moe_unit(m, c):
                    m += MOE_UNITS * j
                    pe.wait_ge(lo_done, U_MOE + m + 1 + 2 * MOE_UNITS * it)
                    s = (U_MOE + m) % PARTS
                    return (w_[:, s, :].rearrange("p (c n) -> p c n", c=c) for w_ in (w_hi, w_lo))

                def down(b, m):
                    pe.wait_ge(mhl_done, MOE_BLOCKS * e + (b + 1))
                    if b == 0:
                        pe.wait_ge(acc_done, 4 * e)
                    for a in range(2):
                        h, l = moe_unit(m + a, 2)
                        for cc in range(2):
                            c = 2 * a + cc
                            for i, packed in enumerate(tiles):
                                o = 512 * i + c * P
                                for q in range(2):
                                    last = mm_tile(ps[:, 2 * i + q, :], lambda part: ht[:, part, o:o + P],
                                                   h[:, cc, q * 512:q * 512 + 512], l[:, cc, q * 512:q * 512 + 512],
                                                   packed, b == 0 and c == 0, b == MOE_BLOCKS - 1 and c == 3)
                        last.then_inc(unit_used, 1)

                def h_transpose(b):
                    pe.wait_ge(mh_ok, 2 * (MOE_BLOCKS * e + (b + 1)))
                    for i in range(nt):
                        for c in range(4):
                            last = t_.transpose(ps[:, gate_bank(b, i, nt), c * P:c * P + P],
                                                eh[:, i, c * P:c * P + P], ident[:, :])
                    last.then_inc(mhT_ps, 1)

                m = 0
                for b in range(MOE_BLOCKS):
                    for u in (1, 0):
                        if u == 0:
                            if b == 0:
                                pe.wait_ge(pt_sb, e + 1)
                            elif nt == 2:
                                pe.wait_ge(mhl_done, MOE_BLOCKS * e + b)
                            elif b == 1:
                                h_transpose(0)
                        for a in range(2):
                            h, l = moe_unit(m, 4)
                            for i, packed in enumerate(tiles):
                                for cc in range(4):
                                    c = 4 * a + cc
                                    last = mm_tile(ps[:, gate_bank(b, i, nt) + u, :],
                                                   lambda part: x_tile(part, i, c),
                                                   h[:, cc, :], l[:, cc, :], packed, c == 0, c == KC - 1)
                            last.then_inc(unit_used, 1)
                            m += 1
                    if b:
                        down(b - 1, m)
                        m += 2
                    if nt == 2 or b:
                        h_transpose(b)
                down(MOE_BLOCKS - 1, m)

            pe.wait_ge(routed, 1)
            with pe.Fori(0, NE // 2) as it:
                for j in range(2):
                    e = 2 * it + j
                    kind = pe.value_load(flag[0:1, bass.ds(e, 1)], min_val=0, max_val=len(KINDS) - 1)
                    last_e = pe.value_load(flag[0:1, bass.ds(e + NE, 1)], min_val=0, max_val=2)
                    with pe.If(kind == 0):
                        gather(e, 1)
                    with pe.If(kind > 0):
                        gather(e, 2)
                    for nt in (1, 2):
                        with pe.If(last_e == nt):
                            combine(e - 1, nt)
                    for n, tiles in enumerate(KINDS):
                        with pe.If(kind == n):
                            blocks(e, j, it, tiles)
            last_e = pe.value_load(flag[0:1, 2 * NE:2 * NE + 1], min_val=0, max_val=2)
            for nt in (1, 2):
                with pe.If(last_e == nt):
                    combine(NE - 1, nt)


_INS = ['x', 'norm_mix_pre', 'norm_mix_post', 'norm_ffn_pre', 'norm_ffn_post', 'nsa_conv_w_in', 'cmp_pe',
        'cmp_w1', 'cmp_b1', 'cmp_w2', 'cmp_b2', 'conv_w', 'conv_b', 'conv_ln_g', 'conv_ln_b',
        'nsa_conv_w_out', 'ffn_w_gate', 'ffn_w_up', 'ffn_w_down', 'gmlp_w_in', 'gmlp_ln_g', 'gmlp_ln_b',
        'gmlp_w_s', 'gmlp_b_s', 'gmlp_w_out', 'moe_w_router', 'moe_w_gate', 'moe_w_up', 'moe_w_down']


def kernel(**inputs):
    import numpy as np
    import concourse.bacc as bacc
    from concourse.bass_utils import run_bass_kernel_spmd

    nc = bacc.Bacc("TRN2", target_bir_lowering=False, num_devices=1)
    arrays, args = {}, []
    for name in _INS:
        a = np.ascontiguousarray(inputs[name])
        arrays[f"in_{name}"] = a
        args.append(nc.dram_tensor(f"in_{name}", a.shape, mybir.dt.from_np(a.dtype), kind="ExternalInput").ap())
    args.append(nc.dram_tensor("out", (1, S, D), F32, kind="ExternalOutput").ap())
    program(nc, *args)
    r = run_bass_kernel_spmd(nc, [arrays], core_ids=[0])
    return r.results[0]["out"]
```
